# Optimizing a Trainium2 kernel written in Bass

```python
import jax
import jax.numpy as jnp
from jax import lax
import numpy as np

D_MODEL = 1024
BATCH = 1
SEQ = 256
DEPTH = 1

RET_HEADS = 4
RET_DK = 64
RET_DV = 128
RET_CHUNK = 128
RET_THETA = 10000.0
MOBA_HEADS = 8
MOBA_DH = 64
MOBA_BLOCK = 256
MOBA_TOPK = 3
MOBA_Q_CHUNK = 16
ROPE_THETA = 500000.0
ROPE_DIM = MOBA_DH // 4
RET_QK_W = RET_HEADS * RET_DK
RET_V_W = RET_HEADS * RET_DV
MOBA_W = MOBA_HEADS * MOBA_DH
D_MIX = RET_V_W + MOBA_W
D_IN = 2 * RET_QK_W + 2 * RET_V_W + 3 * MOBA_W
SPLITS = [int(v) for v in np.cumsum([RET_QK_W, RET_QK_W, RET_V_W, RET_V_W, MOBA_W, MOBA_W])]
N_EXPERTS = 32
TOP_K = 4
D_EXPERT = D_MODEL
SWIGLU_LIMIT = 7.0
SWIGLU_ALPHA = 1.702
MOE_BLOCK = 256
RMS_EPS = 1e-5
GN_EPS = 1e-6
NEG_INF = -1e30

kernel_name = "hybrid_retention_moba_moe_layer"

def rms_norm(x, w):
    xf = x.astype(jnp.float32)
    y = xf * lax.rsqrt(jnp.mean(xf * xf, axis=-1, keepdims=True) + RMS_EPS)
    return (y * w.astype(jnp.float32)).astype(x.dtype)

def rotary(x, pos, rot_dim, theta):
    half = rot_dim // 2
    inv_freq = theta ** (-2.0 * jnp.arange(half, dtype=jnp.float32) / rot_dim)
    ang = pos.astype(jnp.float32)[:, None] * inv_freq[None, :]
    cos = jnp.cos(ang)[None, :, None, :]
    sin = jnp.sin(ang)[None, :, None, :]
    xf = x.astype(jnp.float32)
    x1 = xf[..., :half]
    x2 = xf[..., half:rot_dim]
    out = jnp.concatenate([x1 * cos - x2 * sin, x1 * sin + x2 * cos, xf[..., rot_dim:]], axis=-1)
    return out.astype(x.dtype)

def retention(q, k, v):
    b, s, h, dk = q.shape
    dv = v.shape[-1]
    c = RET_CHUNK
    nc = s // c
    to_chunks = lambda t: t.reshape(b, nc, c, h, t.shape[-1]).transpose(0, 3, 1, 2, 4).astype(jnp.float32)
    qc = to_chunks(q)
    kc = to_chunks(k) * (dk ** -0.5)
    vc = to_chunks(v)
    log_g = jnp.log1p(-jnp.exp2(-5.0 - jnp.arange(h, dtype=jnp.float32)))
    idx = jnp.arange(c, dtype=jnp.float32)
    rel = idx[:, None] - idx[None, :]
    decay = jnp.where(rel >= 0, jnp.exp(log_g[:, None, None] * jnp.maximum(rel, 0.0)), 0.0)
    scores = jnp.einsum("bhcnd,bhcmd->bhcnm", qc, kc) * decay[:, None]
    inner = jnp.einsum("bhcnm,bhcme->bhcne", scores, vc)
    zeta = jnp.exp(log_g[:, None] * (c - 1.0 - idx))
    chunk_state = jnp.einsum("bhcmd,bhcme->bhcde", kc * zeta[:, None, :, None], vc)
    chunk_decay = jnp.exp(log_g * c)[:, None, None]

    def step(r, u):
        return chunk_decay * r + u, r

    _, r_prev = lax.scan(step, jnp.zeros((b, h, dk, dv), jnp.float32), chunk_state.transpose(2, 0, 1, 3, 4))
    r_prev = r_prev.transpose(1, 2, 0, 3, 4)
    xi = jnp.exp(log_g[:, None] * (idx + 1.0))
    cross = jnp.einsum("bhcnd,bhcde->bhcne", qc * xi[:, None, :, None], r_prev)
    return (inner + cross).transpose(0, 2, 3, 1, 4).reshape(b, s, h, dv)

def moba_attention(q, k, v):
    b, h, s, d = q.shape
    nb = -(-s // MOBA_BLOCK)
    sp = nb * MOBA_BLOCK
    pad = [(0, 0), (0, 0), (0, sp - s), (0, 0)]
    q = jnp.pad(q, pad)
    k = jnp.pad(k, pad)
    v = jnp.pad(v, pad)
    kb = k.reshape(b, h, nb, MOBA_BLOCK, d)
    vb = v.reshape(b, h, nb, MOBA_BLOCK, d)
    k_mean = jnp.mean(kb.astype(jnp.float32), axis=3)
    gate = jnp.einsum("bhsd,bhnd->bhsn", q.astype(jnp.float32), k_mean)
    q_blk = jnp.arange(sp) // MOBA_BLOCK
    fully_past = jnp.arange(nb)[None, :] < q_blk[:, None]
    gate = jnp.where(fully_past, gate, NEG_INF)
    k_sel = max(1, min(MOBA_TOPK, nb - 1))
    _, sel = lax.top_k(gate, k_sel)
    nq = sp // MOBA_Q_CHUNK
    qs = q.reshape(b, h, nq, MOBA_Q_CHUNK, d).transpose(2, 0, 1, 3, 4)
    sels = sel.reshape(b, h, nq, MOBA_Q_CHUNK, k_sel).transpose(2, 0, 1, 3, 4)
    gather = jax.vmap(jax.vmap(lambda blocks, ids: blocks[ids]))
    scale = d ** -0.5
    key_in_blk = jnp.arange(MOBA_BLOCK)
    slot_ids = jnp.arange(k_sel)

    def query_chunk(args):
        ci, q_c, sel_c = args
        q0 = ci * MOBA_Q_CHUNK
        blk = q0 // MOBA_BLOCK
        k_own = lax.dynamic_index_in_dim(kb, blk, axis=2, keepdims=False)
        v_own = lax.dynamic_index_in_dim(vb, blk, axis=2, keepdims=False)
        k_g = gather(kb, sel_c)
        v_g = gather(vb, sel_c)
        s_own = jnp.einsum("bhqd,bhld->bhql", q_c, k_own, preferred_element_type=jnp.float32) * scale
        q_in_blk = q0 % MOBA_BLOCK + jnp.arange(MOBA_Q_CHUNK)
        s_own = jnp.where(key_in_blk[None, :] <= q_in_blk[:, None], s_own, NEG_INF)
        s_sel = jnp.einsum("bhqd,bhqkld->bhqkl", q_c, k_g, preferred_element_type=jnp.float32) * scale
        s_sel = jnp.where((slot_ids < blk)[:, None], s_sel, NEG_INF)
        n_sel = k_sel * MOBA_BLOCK
        logits = jnp.concatenate([s_sel.reshape(b, h, MOBA_Q_CHUNK, n_sel), s_own], axis=-1)
        p = jax.nn.softmax(logits, axis=-1)
        p_sel = p[..., :n_sel].reshape(b, h, MOBA_Q_CHUNK, k_sel, MOBA_BLOCK).astype(v.dtype)
        p_own = p[..., n_sel:].astype(v.dtype)
        return (jnp.einsum("bhqkl,bhqkld->bhqd", p_sel, v_g, preferred_element_type=jnp.float32)
                + jnp.einsum("bhql,bhld->bhqd", p_own, v_own, preferred_element_type=jnp.float32))

    out = lax.map(query_chunk, (jnp.arange(nq), qs, sels))
    return out.transpose(1, 2, 0, 3, 4).reshape(b, h, sp, d)[:, :, :s]

def clamped_swiglu(u):
    gate, lin = jnp.split(u, 2, axis=-1)
    gate = jnp.minimum(gate, SWIGLU_LIMIT)
    lin = jnp.clip(lin, -SWIGLU_LIMIT, SWIGLU_LIMIT)
    return gate * jax.nn.sigmoid(SWIGLU_ALPHA * gate) * (lin + 1.0)

def moe_ffn(h, w_router, b_router, w1, b1, w2, b2):
    n, d = h.shape
    logits = jnp.dot(h, w_router, preferred_element_type=jnp.float32) + b_router.astype(jnp.float32)
    top_logit, top_e = lax.top_k(logits, TOP_K)
    gate = jax.nn.softmax(top_logit, axis=-1)
    n_pairs = n * TOP_K
    e_flat = top_e.reshape(n_pairs)
    order = jnp.argsort(e_flat).astype(jnp.int32)
    e_sorted = e_flat[order]
    counts = jnp.bincount(e_flat, length=N_EXPERTS).astype(jnp.int32)
    padded = (counts + MOE_BLOCK - 1) // MOE_BLOCK * MOE_BLOCK
    start = jnp.cumsum(counts) - counts
    pad_end = jnp.cumsum(padded)
    pad_start = pad_end - padded
    dest = pad_start[e_sorted] + jnp.arange(n_pairs, dtype=jnp.int32) - start[e_sorted]
    n_blocks = -(-n_pairs // MOE_BLOCK) + N_EXPERTS
    slot_pair = jnp.full((n_blocks * MOE_BLOCK,), n_pairs, dtype=jnp.int32).at[dest].set(order)
    slot_tok = slot_pair // TOP_K
    slot_gate = jnp.concatenate([gate.reshape(n_pairs), jnp.zeros((1,), gate.dtype)])[slot_pair]
    block_expert = jnp.minimum(
        jnp.searchsorted(pad_end, jnp.arange(n_blocks, dtype=jnp.int32) * MOE_BLOCK, side="right"),
        N_EXPERTS - 1)
    h_pad = jnp.concatenate([h, jnp.zeros((1, d), h.dtype)], axis=0)

    def expert_block(acc, xs):
        tok, g, e = xs
        u = jnp.dot(h_pad[tok], w1[e], preferred_element_type=jnp.float32) + b1[e]
        y = jnp.dot(clamped_swiglu(u).astype(h.dtype), w2[e], preferred_element_type=jnp.float32) + b2[e]
        return acc.at[tok].add(y * g[:, None]), None

    acc, _ = lax.scan(expert_block, jnp.zeros((n + 1, d), jnp.float32),
                      (slot_tok.reshape(n_blocks, MOE_BLOCK), slot_gate.reshape(n_blocks, MOE_BLOCK), block_expert))
    return acc[:n].astype(h.dtype)

def setup_inputs(seed: int = 0) -> dict:
    key = jax.random.key(seed)
    ks = jax.random.split(key, 13)
    f32 = jnp.float32
    nrm = lambda k, shape, scale: jax.random.normal(k, shape, f32) * scale
    return {
        "x": nrm(ks[0], (BATCH, SEQ, D_MODEL), 1.0),
        "norm1_w": 1.0 + nrm(ks[1], (DEPTH, D_MODEL), 0.02),
        "w_in": nrm(ks[2], (DEPTH, D_MODEL, D_IN), D_MODEL ** -0.5),
        "ret_norm_w": 1.0 + nrm(ks[3], (DEPTH, RET_V_W), 0.02),
        "w_out": nrm(ks[4], (DEPTH, D_MIX, D_MODEL), D_MIX ** -0.5),
        "norm2_w": 1.0 + nrm(ks[5], (DEPTH, D_MODEL), 0.02),
        "w_router": nrm(ks[6], (DEPTH, D_MODEL, N_EXPERTS), D_MODEL ** -0.5),
        "b_router": nrm(ks[7], (DEPTH, N_EXPERTS), 0.01),
        "w1": nrm(ks[8], (DEPTH, N_EXPERTS, D_MODEL, 2 * D_EXPERT), D_MODEL ** -0.5),
        "b1": nrm(ks[9], (DEPTH, N_EXPERTS, 2 * D_EXPERT), 0.01),
        "w2": nrm(ks[10], (DEPTH, N_EXPERTS, D_EXPERT, D_MODEL), D_EXPERT ** -0.5),
        "b2": nrm(ks[11], (DEPTH, N_EXPERTS, D_MODEL), 0.01),
        "final_norm_w": 1.0 + nrm(ks[12], (D_MODEL,), 0.02),
    }

def reference(x, norm1_w, w_in, ret_norm_w, w_out, norm2_w, w_router, b_router, w1, b1, w2, b2, final_norm_w):
    b, s, d = x.shape
    pos = jnp.arange(s)
    for i in range(DEPTH):
        h = rms_norm(x, norm1_w[i])
        proj = jnp.dot(h, w_in[i])
        rq, rk, rv, rg, mq, mk, mv = jnp.split(proj, SPLITS, axis=-1)
        rq = rotary(rq.reshape(b, s, RET_HEADS, RET_DK), pos, RET_DK, RET_THETA)
        rk = rotary(rk.reshape(b, s, RET_HEADS, RET_DK), pos, RET_DK, RET_THETA)
        ret = retention(rq, rk, rv.reshape(b, s, RET_HEADS, RET_DV))
        mu = jnp.mean(ret, axis=-1, keepdims=True)
        var = jnp.mean(jnp.square(ret - mu), axis=-1, keepdims=True)
        ret = ((ret - mu) * lax.rsqrt(var + GN_EPS)).reshape(b, s, RET_V_W) * ret_norm_w[i].astype(jnp.float32)
        ret = (jax.nn.silu(rg.astype(jnp.float32)) * ret).astype(x.dtype)
        mq = rotary(mq.reshape(b, s, MOBA_HEADS, MOBA_DH), pos, ROPE_DIM, ROPE_THETA).transpose(0, 2, 1, 3)
        mk = rotary(mk.reshape(b, s, MOBA_HEADS, MOBA_DH), pos, ROPE_DIM, ROPE_THETA).transpose(0, 2, 1, 3)
        mv = mv.reshape(b, s, MOBA_HEADS, MOBA_DH).transpose(0, 2, 1, 3)
        moba = moba_attention(mq, mk, mv).transpose(0, 2, 1, 3).reshape(b, s, MOBA_W).astype(x.dtype)
        x = x + jnp.dot(jnp.concatenate([ret, moba], axis=-1), w_out[i])
        h2 = rms_norm(x, norm2_w[i]).reshape(b * s, d)
        x = x + moe_ffn(h2, w_router[i], b_router[i], w1[i], b1[i], w2[i], b2[i]).reshape(b, s, d)
    return rms_norm(x, final_norm_w)


_drawn_inputs = setup_inputs


def setup_inputs(seed=0):
    import zlib

    import numpy as np

    out = dict(_drawn_inputs(seed))
    spreads = {}
    factors = {'b1': 8.0, 'b2': 8.0, 'final_norm_w': 2.884}
    for name, (base, spread) in spreads.items():
        noise = np.random.default_rng([zlib.crc32(name.encode()), seed]).standard_normal(out[name].shape)
        drawn = base * np.exp(spread * noise) if base else spread * noise
        out[name] = jnp.asarray(drawn.astype(out[name].dtype))
    for name, factor in factors.items():
        out[name] = (out[name] * factor).astype(out[name].dtype)
    return out
```

```python
import concourse.bass as bass
from concourse import mybir
from contextlib import ExitStack

F32 = mybir.dt.float32
I32 = mybir.dt.int32
U32 = mybir.dt.uint32
ALU = mybir.AluOpType
ACT = mybir.ActivationFunctionType
AX = mybir.AxisListType

P = 128
SEQ = 256
T = SEQ // P
D = 1024
C = D // P
RET_HEADS, RET_DK, RET_DV = 4, 64, 128
MOBA_HEADS, MOBA_DH, MOBA_ROPE = 8, 64, 16
D_IN = 3072
E = 32
TOPK = 4
F = 1024
SLOTS = 64
ROUNDS = SEQ // SLOTS
BANK = 512
LIMIT, ALPHA = 7.0, 1.702
RMS_EPS, GN_EPS = 1e-5, 1e-6

RING = 16
SLOT_COLS = 2048
WIN_COLS = SLOT_COLS // C
WIN_CHUNKS = D_IN // WIN_COLS
WOUT_CHUNKS = C // 2
HEAD_CHUNKS = WIN_CHUNKS + WOUT_CHUNKS
W1_CHUNKS = C
W2_CHUNKS = C // 2
EXPERT_CHUNKS = W1_CHUNKS + W2_CHUNKS
UNROLL = 4
ITERS = E // UNROLL
assert HEAD_CHUNKS == RING and (UNROLL * EXPERT_CHUNKS) % RING == 0
TURNS = UNROLL * EXPERT_CHUNKS // RING

RQ, RK, RV, RG, MQ, MK, MV = 0, 256, 512, 1024, 1536, 2048, 2560
CHUNK_COL = [MQ, MK, MQ + 256, MK + 256, MV, MV + 256, RQ, RK, RV, RV + 256, RG, RG + 256]
WOUT_ORDER = [2, 3, 0, 1]

CONST_PARTS = [("ident", P), ("before", P), ("ones", P), ("causal", P), ("decay", RET_HEADS * SEQ),
               ("slot", 2 * SLOTS), ("expert", E), ("ret_cos", T * RET_DK), ("ret_sin", T * RET_DK),
               ("moba_cos", T * MOBA_ROPE), ("moba_sin", T * MOBA_ROPE)]
CONST_COLS = sum(n for _, n in CONST_PARTS)


def layer_kernel(nc, x, norm1_w, w_in, ret_norm_w, w_out, norm2_w, w_router, b_router,
                 w1, b1, w2, b2, final_norm_w, consts, out):
    x_v = x.rearrange("b (t p) d -> p (b t) d", p=P)
    out_v = out.rearrange("b (t p) d -> p (b t) d", p=P)
    win_v = w_in.rearrange("l (c p) n -> p (l c) n", p=P)
    wout_v = w_out.rearrange("l (c p) n -> p (l c) n", p=P)
    w1_v = w1.rearrange("l e (c p) n -> (l e) c p n", p=P)
    w2_v = w2.rearrange("l e (c p) n -> (l e) p c n", p=P)

    ctx = ExitStack()
    with ctx:
        def sb(name, shape, dt=F32):
            return ctx.enter_context(nc.sbuf_tensor(name, shape, dt))

        def sem(name):
            return ctx.enter_context(nc.semaphore(name))

        ctx.enter_context(nc.allow_non_contiguous_dma(reason="norm weights, one element per partition and tile"))
        PS = ctx.enter_context(nc.psum_tensor("PS", [P, 8 * BANK], F32))

        def bank(b, n=1):
            return PS[:, b * BANK:(b + n) * BANK]

        ring = sb("ring", [P, RING, SLOT_COLS])
        cst = sb("cst", [P, CONST_COLS])
        resid = sb("resid", [P, T, D])
        nat = sb("nat", [P, T, D_IN])
        nat_flat = nat[:, :, :].rearrange("p t n -> p (t n)")
        hT = sb("hT", [P, T, C, P])
        mixT = sb("mixT", [P, C, SEQ])
        work = sb("work", [P, 12 * SEQ + 4 * 3 * P])
        n1w = sb("n1w", [P, C])
        n2w = sb("n2w", [P, C])
        br = sb("br", [1, E])
        wr = sb("wr", [P, C, E])
        stat = sb("stat", [P, 64])
        bn = sb("bn", [P, T * RET_HEADS, 6])
        gn = sb("gn", [P, T * RET_HEADS, 2])
        gn_rstd = sb("gn_rstd", [P, T * RET_HEADS])
        logits = sb("logits", [P, T, E])
        top = sb("top", [P, T, 8])
        top_i = sb("top_i", [P, T, 8], U32)
        top_f = sb("top_f", [P, T, 8])
        gate4 = sb("gate4", [P, T, TOPK])
        gates = sb("gates", [P, T, E + 1])
        member = sb("member", [P, T, E])
        place = sb("place", [P, T, E + 1])
        gatesT = sb("gatesT", [E, SEQ])
        most = sb("most", [P, 1])
        most_i = sb("most_i", [1, 1], I32)

        c_at, at = {}, 0
        for name, n in CONST_PARTS:
            c_at[name] = cst[:, at:at + n]
            at += n
        ident, before, ones, causal = (c_at[n] for n in ("ident", "before", "ones", "causal"))
        decay = c_at["decay"].rearrange("p (h n) -> p h n", h=RET_HEADS)
        slot_id = c_at["slot"]
        expert_id = c_at["expert"]
        ret_cos = c_at["ret_cos"].rearrange("p (t d) -> p t d", t=T)
        ret_sin = c_at["ret_sin"].rearrange("p (t d) -> p t d", t=T)
        moba_cos = c_at["moba_cos"].rearrange("p (t d) -> p t d", t=T)
        moba_sin = c_at["moba_sin"].rearrange("p (t d) -> p t d", t=T)

        xn = mixT[:, :, :].rearrange("p c n -> p (c n)").rearrange("p (t d) -> p t d", t=T)
        qkT = work[:, 0:12 * SEQ].rearrange("p (i n) -> p i n", n=SEQ)
        prob = work[:, 3072:3840].rearrange("p (s n) -> p s n", s=2)
        probT = work[:, 3840:4608].rearrange("p (s n) -> p s n", s=2)
        decayed = prob
        retw = nat[:, 0, MQ:MQ + 512]
        ret = nat[:, :, RQ:RQ + 512]

        h2n = hT[:, :, :, :].rearrange("p t c n -> p t (c n)")
        h2T = nat_flat[:, 0:2048].rearrange("p (t c n) -> p t c n", t=T, c=C)
        b1_sb = nat_flat[0:E, 2048:4096]
        b2_sb = nat_flat[0:E, 4096:5120]
        fnw = nat_flat[:, 5120:6144]
        gh = work[:, 0:512].rearrange("p (c s) -> p c s", c=C)
        pick = work[:, 512:640].rearrange("p (t s) -> p t s", t=T)
        pickg = work[:, 640:896].rearrange("p (t s) -> p t s", t=T)
        putb = work[:, 896:1408].rearrange("p (b n) -> p b n", b=2)
        bsel = work[0:E, 1408:1536].rearrange("p (b n) -> p b n", b=2)
        g_sb = work[:, 1536:2048]
        l_sb = work[:, 2048:2560]
        s_sb = work[:, 2560:3072]
        a_sb = work[:, 3072:3584]
        aT = work[:, 3584:4096].rearrange("p (c n) -> p c n", c=4)
        y_sb = work[:, 4096:4608]

        scr = sb("scr", [P, 256])
        gsig = nat[:, :, MK:MK + 512]
        dump = mixT[:, :, :].rearrange("p c n -> p (c n)")[:, 0:D]

        slot_full = [sem(f"slot_full{s}") for s in range(RING)]
        chunk_used = sem("chunk_used")
        x_in = [sem(f"x_in{t}") for t in range(T)]
        cst_in = sem("cst_in")
        small_in = sem("small_in")
        retw_in = sem("retw_in")
        late_in = sem("late_in")
        out_done = sem("out_done")
        sumsq_ready = sem("sumsq_ready")
        var_ready = sem("var_ready")
        std_ready = sem("std_ready")
        rstd_ready = sem("rstd_ready")
        xn_ready = sem("xn_ready")
        xT_done = sem("xT_done")
        hT_ready = sem("hT_ready")
        nat_ready = sem("nat_ready")
        roped = sem("roped")
        qkT_done = sem("qkT_done")
        qkT_ready = sem("qkT_ready")
        score_done = sem("score_done")
        masked = sem("masked")
        negmax_ready = sem("negmax_ready")
        exp_ready = sem("exp_ready")
        prob_ready = sem("prob_ready")
        probT_done = sem("probT_done")
        probT_ready = sem("probT_ready")
        pv_done = sem("pv_done")
        pv_taken = sem("pv_taken")
        rscore_done = sem("rscore_done")
        decayed_ready = sem("decayed_ready")
        ret_done = sem("ret_done")
        siglu_ready = sem("siglu_ready")
        gnvar_ready = sem("gnvar_ready")
        gnstd_ready = sem("gnstd_ready")
        ret_ready = sem("ret_ready")
        retT_done = sem("retT_done")
        retT_ready = sem("retT_ready")
        wout_done = sem("wout_done")
        x2_ready = sem("x2_ready")
        h2n_ready = sem("h2n_ready")
        h2T_done = sem("h2T_done")
        h2T_ready = sem("h2T_ready")
        logits_done = sem("logits_done")
        top_ready = sem("top_ready")
        topexp_ready = sem("topexp_ready")
        member_ready = sem("member_ready")
        prefix_done = sem("prefix_done")
        gatesT_done = sem("gatesT_done")
        gatesT_ready = sem("gatesT_ready")
        place_ready = sem("place_ready")
        most_ready = sem("most_ready")
        dve_step = sem("dve_step")
        prep_ready = sem("prep_ready")
        put_done = sem("put_done")
        put_ready = sem("put_ready")
        gather_done = sem("gather_done")
        gh_ready = sem("gh_ready")
        gate_ready = sem("gate_ready")
        lin_ready = sem("lin_ready")
        glin_ready = sem("glin_ready")
        sig_ready = sem("sig_ready")
        act_ready = sem("act_ready")
        actT_done = sem("actT_done")
        actT_ready = sem("actT_ready")
        y_ready = sem("y_ready")
        combined = sem("combined")
        final_ready = sem("final_ready")
        outrow_ready = sem("outrow_ready")

        def slot_of(u, k):
            g = EXPERT_CHUNKS * u + k
            return g % RING, g // RING

        def up_done(n):
            return n * EXPERT_CHUNKS + (HEAD_CHUNKS + W1_CHUNKS)

        def down_done(n):
            return n * EXPERT_CHUNKS + (HEAD_CHUNKS + EXPERT_CHUNKS)

        block = ctx.enter_context(nc.Block())

        @block.sync
        def _(sp):
            for t in range(T):
                sp.dma_start(resid[:, t, :], x_v[:, t, :]).then_inc(x_in[t], 16)
            for j, col in enumerate(CHUNK_COL):
                dst = ring[:, j, :].rearrange("p (c n) -> p c n", c=C)
                sp.dma_start(dst, win_v[:, :, col:col + WIN_COLS]).then_inc(slot_full[j], 16)
            for j, pair in enumerate(WOUT_ORDER):
                s = WIN_CHUNKS + j
                dst = ring[:, s, :].rearrange("p (c n) -> p c n", c=2)
                sp.dma_start(dst, wout_v[:, 2 * pair:2 * pair + 2, :]).then_inc(slot_full[s], 16)

            def expert_loads(n, e, u):
                for k in range(EXPERT_CHUNKS):
                    s, _ = slot_of(u, k)
                    sp.wait_ge(chunk_used, n * EXPERT_CHUNKS + (k + 1))
                    if k < W1_CHUNKS:
                        sp.dma_start(ring[:, s, :], w1_v[e, k, :, :]).then_inc(slot_full[s], 16)
                    else:
                        c = 2 * (k - W1_CHUNKS)
                        dst = ring[:, s, :].rearrange("p (c n) -> p c n", c=2)
                        sp.dma_start(dst, w2_v[e, :, c:c + 2, :]).then_inc(slot_full[s], 16)

            with sp.Fori(0, ITERS) as i:
                for u in range(UNROLL):
                    expert_loads(i * UNROLL + u, i * UNROLL + u, u)
            sp.wait_ge(most_ready, 1)
            most_v = sp.value_load(most_i[0:1, 0:1], min_val=0, max_val=SEQ)
            with sp.If(most_v > SLOTS):
                with sp.Fori(1, ROUNDS) as r:
                    with sp.Fori(0, ITERS) as i:
                        for u in range(UNROLL):
                            expert_loads(r * E + i * UNROLL + u, i * UNROLL + u, u)
            for t in range(T):
                sp.wait_ge(outrow_ready, t + 1)
                sp.dma_start(out_v[:, t, :], resid[:, t, :]).then_inc(out_done, 16)
            sp.wait_ge(out_done, 16 * T)

        @block.gpsimd
        def _(pool):
            pool.wait_ge(qkT_done, 4)
            pool.dma_start(retw, ret_norm_w.broadcast_to([P, 512])).then_inc(retw_in, 16)
            pool.wait_ge(retT_done, 2)
            pool.wait_ge(pv_taken, 4)
            pool.dma_start(b1_sb, b1[0, :, :]).then_inc(late_in, 16)
            pool.dma_start(b2_sb, b2[0, :, :]).then_inc(late_in, 16)
            pool.dma_start(fnw, final_norm_w.rearrange("(a n) -> a n", a=1).broadcast_to([P, D])).then_inc(late_in, 16)
            pool.wait_ge(late_in, 48)

        @block.scalar
        def _(act):
            act.dma_start(cst[:, :], consts).then_inc(cst_in, 16)
            act.dma_start(n1w[:, :], norm1_w.rearrange("l (c p) -> p (l c)", p=P)).then_inc(small_in, 16)
            act.dma_start(n2w[:, :], norm2_w.rearrange("l (c p) -> p (l c)", p=P)).then_inc(small_in, 16)
            act.dma_start(br[:, :], b_router).then_inc(small_in, 16)
            act.dma_start(wr[:, :, :], w_router.rearrange("l (c p) n -> p (l c) n", p=P)).then_inc(small_in, 16)

            for t in range(T):
                act.wait_ge(x_in[t], 16)
                if t:
                    act.wait_ge(sumsq_ready, t)
                nc.scalar.activation(dump, resid[:, t, :], ACT.Square, scale=1.0 / 32.0,
                                     accum_out=stat[:, t:t + 1]).then_inc(sumsq_ready, 1)
            act.wait_ge(var_ready, 1)
            nc.scalar.activation(stat[:, 4:6], stat[:, 2:4], ACT.Sqrt).then_inc(std_ready, 1)

            def take_proj(j, func=ACT.Copy):
                act.wait_ge(chunk_used, j + 1)
                col = CHUNK_COL[j]
                nc.scalar.activation(nat[:, :, col:col + WIN_COLS],
                                     bank(4 + j % 2).rearrange("p (t n) -> p t n", t=T), func).then_inc(nat_ready, 1)

            def exps(g):
                for h in (2 * g, 2 * g + 1):
                    act.wait_ge(negmax_ready, h + 1)
                    for t, (a, b) in enumerate(((0, P), (P, 3 * P))):
                        nc.scalar.activation(prob[:, h % 2, a:b], prob[:, h % 2, a:b], ACT.Exp,
                                             bias=stat[:, 8 + 2 * (h % 2) + t:9 + 2 * (h % 2) + t],
                                             scale=MOBA_DH ** -0.5,
                                             accum_out=stat[:, 12 + 2 * (h % 2) + t:13 + 2 * (h % 2) + t]
                                             ).then_inc(exp_ready, 1)

            for j in range(6):
                take_proj(j)
            exps(0)
            take_proj(6)
            exps(1)
            take_proj(7)
            exps(2)
            take_proj(8)
            exps(3)
            take_proj(9)
            take_proj(10)
            take_proj(11)
            act.wait_ge(nat_ready, WIN_CHUNKS)
            for t in range(T):
                nc.scalar.activation(gsig[:, t, :], nat[:, t, RG:RG + 512], ACT.Sigmoid).then_inc(siglu_ready, 1)
            act.wait_ge(gnvar_ready, 1)
            nc.scalar.activation(gn_rstd[:, :], gn_rstd[:, :], ACT.Sqrt).then_inc(gnstd_ready, 1)
            for t in range(T):
                act.wait_ge(x2_ready, t + 1)
                act.wait_ge(sumsq_ready, T + t)
                nc.scalar.activation(h2n[:, t, :], resid[:, t, :], ACT.Square, scale=1.0 / 32.0,
                                     accum_out=stat[:, t:t + 1]).then_inc(sumsq_ready, 1)
                act.wait_ge(var_ready, 2 + t)
                nc.scalar.activation(stat[:, 4 + t:5 + t], stat[:, 2 + t:3 + t], ACT.Sqrt).then_inc(std_ready, 1)
            for t in range(T):
                act.wait_ge(top_ready, t + 1)
                nc.scalar.activation(gate4[:, t, :], top[:, t, 0:TOPK], ACT.Exp, bias=stat[:, 20 + t:21 + t],
                                     accum_out=stat[:, 24 + t:25 + t]).then_inc(topexp_ready, 1)

            def expert_act(n):
                act.wait_ge(gate_ready, n + 1)
                nc.scalar.activation(s_sb, g_sb, ACT.Sigmoid, scale=ALPHA).then_inc(sig_ready, 1)
                act.wait_ge(actT_done, n + 1)
                nc.scalar.activation(aT, bank(5).rearrange("p (c n) -> p c n", c=4), ACT.Copy).then_inc(actT_ready, 1)
                act.wait_ge(chunk_used, down_done(n))
                nc.scalar.activation(y_sb, bank(5), ACT.Copy).then_inc(y_ready, 1)

            with act.Fori(0, ITERS) as i:
                for u in range(UNROLL):
                    expert_act(i * UNROLL + u)
            act.wait_ge(most_ready, 1)
            most_v = act.value_load(most_i[0:1, 0:1], min_val=0, max_val=SEQ)
            with act.If(most_v > SLOTS):
                with act.Fori(1, ROUNDS) as r:
                    with act.Fori(0, ITERS) as i:
                        for u in range(UNROLL):
                            expert_act(r * E + i * UNROLL + u)
            for t in range(T):
                act.wait_ge(final_ready, t + 1)
                act.wait_ge(sumsq_ready, 2 * T + t)
                nc.scalar.activation(h2n[:, t, :], resid[:, t, :], ACT.Square, scale=1.0 / 32.0,
                                     accum_out=stat[:, t:t + 1]).then_inc(sumsq_ready, 1)
                act.wait_ge(var_ready, 4 + t)
                nc.scalar.activation(stat[:, 4 + t:5 + t], stat[:, 2 + t:3 + t], ACT.Sqrt).then_inc(std_ready, 1)

        @block.vector
        def _(dve):
            steps = [0]

            def link(ins):
                steps[0] += 1
                ins.then_inc(dve_step, 1)
                dve.wait_ge(dve_step, steps[0])

            nc.vector.memset(gates[:, :, :], 0.0)
            link(nc.vector.memset(place[:, :, :], -1.0))
            dve.wait_ge(sumsq_ready, T)
            nc.vector.tensor_scalar(stat[:, 2:4], stat[:, 0:2], RMS_EPS, None, ALU.add).then_inc(var_ready, 1)
            dve.wait_ge(std_ready, 1)
            link(nc.vector.reciprocal(stat[:, 6:8], stat[:, 4:6]))
            for t in range(T):
                nc.vector.tensor_scalar(xn[:, t, :], resid[:, t, :], stat[:, 6 + t:7 + t], None,
                                        ALU.mult).then_inc(xn_ready, 1)
            dve.wait_ge(small_in, 64)
            dve.wait_ge(cst_in, 16)

            def w_cols(w, c0):
                return w[:, c0:c0 + 4].unsqueeze(2).broadcast_to([P, 4, P])

            for b in range(4):
                t, c0 = b // 2, 4 * (b % 2)
                dve.wait_ge(xT_done, b + 1)
                nc.vector.tensor_tensor(hT[:, t, c0:c0 + 4, :], bank(b).rearrange("p (c n) -> p c n", c=4),
                                        w_cols(n1w, c0), ALU.mult).then_inc(hT_ready, 1)

            rotations = [0]

            def rope(j):
                dve.wait_ge(nat_ready, j + 1)
                if rotations[0]:
                    dve.wait_ge(roped, rotations[0])
                rotations[0] += 1
                retention = CHUNK_COL[j] in (RQ, RK)
                dim = RET_DK if retention else MOBA_ROPE
                cos, sin = (ret_cos, ret_sin) if retention else (moba_cos, moba_sin)
                half, heads = dim // 2, WIN_COLS // 64
                for t in range(T):
                    v = nat[:, t, CHUNK_COL[j]:CHUNK_COL[j] + WIN_COLS].rearrange("p (h d) -> p h d", h=heads)
                    swapped = scr[:, 0:heads * dim].rearrange("p (h d) -> p h d", h=heads)

                    def table(tab, a, b):
                        return tab[:, t, a:b].unsqueeze(1).broadcast_to([P, heads, b - a])

                    nc.vector.tensor_tensor(swapped[:, :, 0:half], v[:, :, half:dim], table(sin, 0, half), ALU.mult)
                    link(nc.vector.tensor_tensor(swapped[:, :, half:dim], v[:, :, 0:half], table(sin, half, dim),
                                                 ALU.mult))
                    link(nc.vector.tensor_tensor(v[:, :, 0:dim], v[:, :, 0:dim], table(cos, 0, dim), ALU.mult))
                    ins = nc.vector.tensor_tensor(v[:, :, 0:dim], v[:, :, 0:dim], swapped, ALU.add)
                    if t == 0:
                        link(ins)
                ins.then_inc(roped, 1)

            def take_qkT(i, tile):
                dve.wait_ge(qkT_done, i + 1)
                nc.vector.tensor_copy(qkT[:, tile:tile + 2, :],
                                      bank(6).rearrange("p (i n) -> p i n", i=2)).then_inc(qkT_ready, 1)

            def mask_max(g):
                for h in (2 * g, 2 * g + 1):
                    s = bank(h % 2)
                    diag = s[:, 0:3 * P].rearrange("p (b n) -> p b n", b=3)[:, 0:3:2, :]
                    pdiag = prob[:, h % 2, :].rearrange("p (b n) -> p b n", b=3)[:, 0:3:2, :]
                    dve.wait_ge(score_done, h + 1)
                    nc.vector.tensor_tensor(pdiag, diag, causal.unsqueeze(1).broadcast_to([P, 2, P]), ALU.add)
                    nc.vector.tensor_copy(prob[:, h % 2, P:2 * P], s[:, P:2 * P]).then_inc(masked, 1)
                    dve.wait_ge(masked, h + 1)
                    if h >= 2:
                        dve.wait_ge(negmax_ready, h - 1)
                    m = stat[:, 16 + 2 * (h % 2):18 + 2 * (h % 2)]
                    nc.vector.reduce_max(m[:, 0:1], prob[:, h % 2, 0:P], AX.X)
                    link(nc.vector.reduce_max(m[:, 1:2], prob[:, h % 2, P:3 * P], AX.X))
                    nc.vector.tensor_scalar(stat[:, 8 + 2 * (h % 2):10 + 2 * (h % 2)], m, -MOBA_DH ** -0.5, None,
                                            ALU.mult).then_inc(negmax_ready, 1)

            def normalise(g):
                for h in (2 * g, 2 * g + 1):
                    dve.wait_ge(exp_ready, 2 * h + 2)
                    if h >= 2:
                        dve.wait_ge(prob_ready, h - 1)
                    r = stat[:, 28 + 2 * (h % 2):30 + 2 * (h % 2)]
                    link(nc.vector.reciprocal(r, stat[:, 12 + 2 * (h % 2):14 + 2 * (h % 2)]))
                    nc.vector.tensor_scalar(prob[:, h % 2, 0:P], prob[:, h % 2, 0:P], r[:, 0:1], None, ALU.mult)
                    nc.vector.tensor_scalar(prob[:, h % 2, P:3 * P], prob[:, h % 2, P:3 * P], r[:, 1:2], None,
                                            ALU.mult).then_inc(prob_ready, 1)

            def take_probT(g):
                for h in (2 * g, 2 * g + 1):
                    dve.wait_ge(probT_done, h + 1)
                    nc.vector.tensor_copy(probT[:, h % 2, :], bank(2 if h % 2 == 0 else 7)[:, 0:3 * P]
                                          ).then_inc(probT_ready, 1)

            def take_pv(g):
                dve.wait_ge(pv_done, g + 1)
                nc.vector.tensor_copy(mixT[:, 4 + g, :], bank(3)[:, 0:SEQ]).then_inc(pv_taken, 1)

            rope(0)
            rope(1)
            take_qkT(0, 4)
            rope(2)
            take_qkT(1, 8)
            rope(3)
            take_qkT(2, 6)
            take_qkT(3, 10)
            mask_max(0)
            normalise(0)
            take_probT(0)
            mask_max(1)
            normalise(1)
            rope(6)
            take_qkT(4, 0)
            take_pv(0)
            take_probT(1)
            mask_max(2)
            normalise(2)
            rope(7)
            take_qkT(5, 2)
            take_pv(1)
            take_probT(2)
            mask_max(3)
            normalise(3)
            take_pv(2)
            take_probT(3)
            take_pv(3)
            for h in range(RET_HEADS):
                dve.wait_ge(rscore_done, h + 1)
                if h >= 2:
                    dve.wait_ge(ret_done, h - 1)
                s = bank(6 + h % 2)
                nc.vector.tensor_tensor(decayed[:, h % 2, 0:SEQ], s[:, 0:SEQ], decay[:, h, :], ALU.mult)
                nc.vector.tensor_tensor(decayed[:, h % 2, SEQ:SEQ + P], s[:, SEQ:SEQ + P], decay[:, h, 0:P],
                                        ALU.mult).then_inc(decayed_ready, 1)
            dve.wait_ge(retw_in, 16)
            dve.wait_ge(nat_ready, WIN_CHUNKS)
            dve.wait_ge(siglu_ready, T)
            for t in range(T):
                link(nc.vector.tensor_tensor(nat[:, t, RG:RG + 512], nat[:, t, RG:RG + 512], gsig[:, t, :], ALU.mult))
                link(nc.vector.tensor_tensor(nat[:, t, RG:RG + 512], nat[:, t, RG:RG + 512], retw, ALU.mult))
            dve.wait_ge(ret_done, RET_HEADS)
            for t in range(T):
                for h in range(RET_HEADS):
                    nc_in = bank(t)[:, h * RET_DV:(h + 1) * RET_DV]
                    ins = nc.vector.bn_stats(bn[:, t * RET_HEADS + h, :], nc_in)
            link(ins)
            for g in range(T * RET_HEADS):
                ins = nc.vector.bn_aggr(gn[:, g, :], bn[:, g, :])
            link(ins)
            nc.vector.tensor_scalar(gn_rstd[:, :], gn[:, :, 1], GN_EPS, None, ALU.add).then_inc(gnvar_ready, 1)
            dve.wait_ge(gnstd_ready, 1)
            link(nc.vector.reciprocal(gn_rstd[:, :], gn_rstd[:, :]))
            for t in range(T):
                for h in range(RET_HEADS):
                    g = t * RET_HEADS + h
                    ins = nc.vector.tensor_scalar(ret[:, t, h * RET_DV:(h + 1) * RET_DV],
                                                  bank(t)[:, h * RET_DV:(h + 1) * RET_DV],
                                                  gn[:, g, 0:1], gn_rstd[:, g:g + 1], ALU.subtract, ALU.mult)
                link(ins)
                nc.vector.tensor_tensor(ret[:, t, :], ret[:, t, :], nat[:, t, RG:RG + 512],
                                        ALU.mult).then_inc(ret_ready, 1)
            for i in range(2):
                dve.wait_ge(retT_done, i + 1)
                nc.vector.tensor_copy(mixT[:, 2 * i:2 * i + 2, :],
                                      bank(4 + i).rearrange("p (i n) -> p i n", i=2)).then_inc(retT_ready, 1)
            dve.wait_ge(xn_ready, T)
            for t in range(T):
                if t == 0:
                    dve.wait_ge(wout_done, 1)
                else:
                    dve.wait_ge(chunk_used, HEAD_CHUNKS)
                nc.vector.tensor_tensor(resid[:, t, :], resid[:, t, :], bank(2 + 4 * t, 2), ALU.add).then_inc(x2_ready, 1)
                dve.wait_ge(sumsq_ready, T + t + 1)
                nc.vector.tensor_scalar(stat[:, 2 + t:3 + t], stat[:, t:t + 1], RMS_EPS, None,
                                        ALU.add).then_inc(var_ready, 1)
                dve.wait_ge(std_ready, 2 + t)
                link(nc.vector.reciprocal(stat[:, 6 + t:7 + t], stat[:, 4 + t:5 + t]))
                nc.vector.tensor_scalar(h2n[:, t, :], resid[:, t, :], stat[:, 6 + t:7 + t], None,
                                        ALU.mult).then_inc(h2n_ready, 1)
            for b in range(4):
                t, c0 = b // 2, 4 * (b % 2)
                dve.wait_ge(h2T_done, b + 1)
                nc.vector.tensor_tensor(h2T[:, t, c0:c0 + 4, :],
                                        bank((0, 1, 4, 5)[b]).rearrange("p (c n) -> p c n", c=4),
                                        w_cols(n2w, c0), ALU.mult).then_inc(h2T_ready, 1)
            for t in range(T):
                dve.wait_ge(logits_done, t + 1)
                link(nc.vector.tensor_copy(logits[:, t, :], bank(3 + 4 * t)[:, 0:E]))
                link(nc.vector.max(top[:, t, :], logits[:, t, :]))
                nc.vector.tensor_scalar(stat[:, 20 + t:21 + t], top[:, t, 0:1], -1.0, None,
                                        ALU.mult).then_inc(top_ready, 1)
                link(nc.vector.max_index(top_i[:, t, :], top[:, t, :], logits[:, t, :]))
                link(nc.vector.tensor_copy(top_f[:, t, :], top_i[:, t, :]))
            dve.wait_ge(roped, rotations[0])
            hot = scr[:, 0:T * TOPK * E].rearrange("p (t k e) -> p t k e", t=T, k=TOPK)
            for t in range(T):
                dve.wait_ge(topexp_ready, t + 1)
                link(nc.vector.reciprocal(stat[:, 26 + t:27 + t], stat[:, 24 + t:25 + t]))
                link(nc.vector.tensor_scalar(gate4[:, t, :], gate4[:, t, :], stat[:, 26 + t:27 + t], None, ALU.mult))
                for k in range(TOPK):
                    ins = nc.vector.tensor_scalar(hot[:, t, k, :], expert_id, top_f[:, t, k:k + 1],
                                                  gate4[:, t, k:k + 1], ALU.is_equal, ALU.mult)
                link(ins)
                link(nc.vector.reduce_sum(gates[:, t, 0:E], hot[:, t, :, :].rearrange("p k e -> p e k"), AX.X))
                nc.vector.tensor_scalar(member[:, t, :], gates[:, t, 0:E], 0.0, None,
                                        ALU.is_gt).then_inc(member_ready, 1)
            dve.wait_ge(prefix_done, 1)
            dve.wait_ge(member_ready, T)
            for t in range(T):
                link(nc.vector.scalar_tensor_tensor(place[:, t, 0:E], bank(2)[:, t * E:(t + 1) * E], 1.0,
                                                    member[:, t, :], ALU.add, ALU.mult))
            link(nc.vector.tensor_scalar(place[:, :, 0:E], place[:, :, 0:E], -1.0, None, ALU.add))
            link(nc.vector.reduce_max(most[:, :], bank(2)[:, T * E:(T + 1) * E], AX.X))
            nc.vector.tensor_copy(most_i[:, :], most[0:1, :]).then_inc(most_ready, 1)
            dve.wait_ge(gatesT_done, 1)
            nc.vector.tensor_copy(gatesT[:, :], bank(6)[0:E, 0:SEQ]).then_inc(gatesT_ready, 1)

            def prepare(m, e, b, first=False):
                if not first:
                    dve.wait_ge(gather_done, m)
                    dve.wait_ge(put_done, m)
                for t in range(T):
                    nc.vector.tensor_scalar(pick[:, t, :], slot_id[:, 0:SLOTS], place[:, t, e], None, ALU.is_equal)
                    nc.vector.tensor_scalar(pickg[:, t, :], slot_id, place[:, t, e], gates[:, t, e],
                                            ALU.is_equal, ALU.mult)
                nc.vector.tensor_copy(bsel[:, b, :], ident[0:E, e].broadcast_to([E, SLOTS])).then_inc(prep_ready, 1)

            def take_put(m, b):
                dve.wait_ge(put_done, m + 1)
                nc.vector.tensor_copy(putb[:, b, :], bank(4)[:, 0:SEQ]).then_inc(put_ready, 1)

            def take_gather(m):
                dve.wait_ge(gather_done, m + 1)
                nc.vector.tensor_tensor(gh, bank(4).rearrange("p (c s) -> p c s", c=C),
                                        n2w[:, :].unsqueeze(2).broadcast_to([P, C, SLOTS]), ALU.mult
                                        ).then_inc(gh_ready, 1)

            def expert_dve(n, m, e, u):
                prepare(m + 1, bass.ds(e + 1, 1), (u + 1) % 2)
                take_put(m + 1, (u + 1) % 2)
                dve.wait_ge(chunk_used, up_done(n))
                nc.vector.tensor_scalar(g_sb, bank(0), LIMIT, None, ALU.min).then_inc(gate_ready, 1)
                nc.vector.tensor_scalar(l_sb, bank(1), LIMIT, -LIMIT, ALU.min, ALU.max).then_inc(lin_ready, 1)
                dve.wait_ge(gate_ready, n + 1)
                dve.wait_ge(lin_ready, n + 1)
                nc.vector.scalar_tensor_tensor(l_sb, l_sb, 1.0, g_sb, ALU.add, ALU.mult).then_inc(glin_ready, 1)
                dve.wait_ge(glin_ready, n + 1)
                dve.wait_ge(sig_ready, n + 1)
                nc.vector.tensor_tensor(a_sb, l_sb, s_sb, ALU.mult).then_inc(act_ready, 1)
                take_gather(m + 1)

            prepare(0, slice(0, 1), 0, first=True)
            take_put(0, 0)
            take_gather(0)
            with dve.Fori(0, ITERS) as i:
                for u in range(UNROLL):
                    n = i * UNROLL + u
                    expert_dve(n, n, n, u)
            dve.wait_ge(most_ready, 1)
            most_v = dve.value_load(most_i[0:1, 0:1], min_val=0, max_val=SEQ)
            with dve.If(most_v > SLOTS):
                with dve.Fori(1, ROUNDS) as r:
                    dve.wait_ge(prep_ready, r * (E + 1))
                    nc.vector.tensor_scalar(place[:, :, :], place[:, :, :], -float(SLOTS), None,
                                            ALU.add).then_inc(place_ready, 1)
                    dve.wait_ge(place_ready, r)
                    dve.wait_ge(gh_ready, r * (E + 1))
                    prepare(r * (E + 1), slice(0, 1), 0)
                    take_put(r * (E + 1), 0)
                    take_gather(r * (E + 1))
                    with dve.Fori(0, ITERS) as i:
                        for u in range(UNROLL):
                            expert_dve(r * E + i * UNROLL + u, r * (E + 1) + i * UNROLL + u, i * UNROLL + u, u)
                dve.wait_ge(combined, ROUNDS * E)
            dve.wait_ge(combined, E)
            dve.wait_ge(h2n_ready, T)
            for t in range(T):
                nc.vector.tensor_tensor(resid[:, t, :], resid[:, t, :], bank(2 + 4 * t, 2), ALU.add).then_inc(final_ready, 1)
            dve.wait_ge(late_in, 48)
            for t in range(T):
                dve.wait_ge(sumsq_ready, 2 * T + t + 1)
                nc.vector.tensor_scalar(stat[:, 2 + t:3 + t], stat[:, t:t + 1], RMS_EPS, None,
                                        ALU.add).then_inc(var_ready, 1)
                dve.wait_ge(std_ready, 4 + t)
                link(nc.vector.reciprocal(stat[:, 6 + t:7 + t], stat[:, 4 + t:5 + t]))
                nc.vector.scalar_tensor_tensor(resid[:, t, :], resid[:, t, :], stat[:, 6 + t:7 + t], fnw,
                                               ALU.mult, ALU.mult).then_inc(outrow_ready, 1)

        @block.tensor
        def _(pe):
            mm = nc.tensor.matmul
            pe.wait_ge(cst_in, 16)
            for b in range(4):
                t, c0 = b // 2, 4 * (b % 2)
                pe.wait_ge(xn_ready, t + 1)
                for c in range(4):
                    last = nc.tensor.transpose(bank(b)[:, c * P:(c + 1) * P], xn[:, t, (c0 + c) * P:(c0 + c + 1) * P],
                                               ident)
                last.then_inc(xT_done, 1)

            def project(j):
                pe.wait_ge(slot_full[j], 16)
                if j >= 2:
                    pe.wait_ge(nat_ready, j - 1)
                w = ring[:, j, :].rearrange("p (c n) -> p c n", c=C)
                for t in range(T):
                    if j == 0:
                        pe.wait_ge(hT_ready, 2 * t + 2)
                    for c in range(C):
                        last = mm(bank(4 + j % 2)[:, t * WIN_COLS:(t + 1) * WIN_COLS], hT[:, t, c, :], w[:, c, :],
                                  start=(c == 0), stop=(c == C - 1))
                last.then_inc(chunk_used, 1)

            def transpose_qk(i, j, nr):
                pe.wait_ge(roped, nr)
                if i:
                    pe.wait_ge(qkT_ready, i)
                for a in range(2):
                    for t in range(T):
                        last = nc.tensor.transpose(bank(6)[:, a * SEQ + t * P:a * SEQ + (t + 1) * P],
                                                   nat[:, t, CHUNK_COL[j] + a * P:CHUNK_COL[j] + (a + 1) * P], ident)
                last.then_inc(qkT_done, 1)

            def scores(g):
                for h in (2 * g, 2 * g + 1):
                    r = slice(64 * (h % 2), 64 * (h % 2) + 64)
                    q, k = qkT[r, 4 + h // 2, :], qkT[r, 8 + h // 2, :]
                    if h >= 2:
                        pe.wait_ge(masked, h - 1)
                    mm(bank(h % 2)[:, 0:P], q[:, 0:P], k[:, 0:P], start=True, stop=True)
                    mm(bank(h % 2)[:, P:3 * P], q[:, P:SEQ], k, start=True, stop=True).then_inc(score_done, 1)

            def transpose_prob(g):
                for h in (2 * g, 2 * g + 1):
                    pe.wait_ge(prob_ready, h + 1)
                    for b in range(3):
                        last = nc.tensor.transpose(bank(2 if h % 2 == 0 else 7)[:, b * P:(b + 1) * P],
                                                   prob[:, h % 2, b * P:(b + 1) * P], ident)
                    last.then_inc(probT_done, 1)

            def prob_v(g):
                pe.wait_ge(nat_ready, 6)
                if g:
                    pe.wait_ge(pv_taken, g)
                for h in (2 * g, 2 * g + 1):
                    pe.wait_ge(probT_ready, h + 1)
                    o = bank(3)[64 * (h % 2):64 * (h % 2) + 64, :]
                    v = nat[:, :, MV + h * MOBA_DH:MV + (h + 1) * MOBA_DH]
                    mm(o[:, 0:P], v[:, 0, :], probT[:, h % 2, 0:P], start=True, stop=True)
                    mm(o[:, P:SEQ], v[:, 0, :], probT[:, h % 2, P:2 * P], start=True, stop=False)
                    last = mm(o[:, P:SEQ], v[:, 1, :], probT[:, h % 2, 2 * P:3 * P], start=False, stop=True)
                last.then_inc(pv_done, 1)

            def ret_scores(h):
                r = slice(64 * (h % 2), 64 * (h % 2) + 64)
                q, k = qkT[r, h // 2, :], qkT[r, 2 + h // 2, :]
                if h >= 2:
                    pe.wait_ge(decayed_ready, h - 1)
                mm(bank(6 + h % 2)[:, 0:SEQ], k[:, 0:P], q, start=True, stop=True)
                mm(bank(6 + h % 2)[:, SEQ:SEQ + P], k[:, P:SEQ], q[:, P:SEQ], start=True,
                   stop=True).then_inc(rscore_done, 1)

            def ret_v(h):
                pe.wait_ge(decayed_ready, h + 1)
                col = slice(h * RET_DV, (h + 1) * RET_DV)
                v = nat[:, :, RV + h * RET_DV:RV + (h + 1) * RET_DV]
                mm(bank(0)[:, col], decayed[:, h % 2, 0:P], v[:, 0, :], start=True, stop=True)
                mm(bank(1)[:, col], decayed[:, h % 2, P:2 * P], v[:, 0, :], start=True, stop=False)
                mm(bank(1)[:, col], decayed[:, h % 2, 2 * P:3 * P], v[:, 1, :], start=False,
                   stop=True).then_inc(ret_done, 1)

            project(0)
            project(1)
            transpose_qk(0, 0, 1)
            project(2)
            transpose_qk(1, 1, 2)
            project(3)
            transpose_qk(2, 2, 3)
            project(4)
            transpose_qk(3, 3, 4)
            project(5)
            pe.wait_ge(qkT_ready, 4)
            scores(0)
            project(6)
            transpose_prob(0)
            scores(1)
            project(7)
            transpose_qk(4, 6, 5)
            prob_v(0)
            transpose_prob(1)
            scores(2)
            project(8)
            transpose_qk(5, 7, 6)
            prob_v(1)
            transpose_prob(2)
            scores(3)
            project(9)
            prob_v(2)
            transpose_prob(3)
            project(10)
            prob_v(3)
            pe.wait_ge(qkT_ready, 6)
            ret_scores(0)
            pe.wait_ge(probT_ready, MOBA_HEADS)
            ret_scores(1)
            project(11)
            pe.wait_ge(masked, MOBA_HEADS)
            ret_v(0)
            ret_v(1)
            ret_scores(2)
            ret_scores(3)

            def wout(s, c, t):
                w = ring[:, WIN_CHUNKS + s, :].rearrange("p (c n) -> p c n", c=2)
                for j in range(2):
                    last = mm(bank(2 + 4 * t + j), mixT[:, c, t * P:(t + 1) * P], w[:, c % 2, j * BANK:(j + 1) * BANK],
                              start=(c == 4), stop=(c == 3))
                return last

            pe.wait_ge(pv_taken, 4)
            ret_v(2)
            ret_v(3)
            for s, pair in enumerate(WOUT_ORDER[0:2]):
                pe.wait_ge(slot_full[WIN_CHUNKS + s], 16)
                for c in (2 * pair, 2 * pair + 1):
                    for t in range(T):
                        last = wout(s, c, t)
                last.then_inc(chunk_used, 1)
            pe.wait_ge(nat_ready, WIN_CHUNKS)
            pe.wait_ge(ret_ready, T)
            for i in range(2):
                for a in range(2):
                    for t in range(T):
                        col = (2 * i + a) * P
                        last = nc.tensor.transpose(bank(4 + i)[:, a * SEQ + t * P:a * SEQ + (t + 1) * P],
                                                   ret[:, t, col:col + P], ident)
                last.then_inc(retT_done, 1)
            pe.wait_ge(retT_ready, 2)
            for s in (2, 3):
                pe.wait_ge(slot_full[WIN_CHUNKS + s], 16)
            for t in range(T):
                for s in (2, 3):
                    for c in (2 * WOUT_ORDER[s], 2 * WOUT_ORDER[s] + 1):
                        last = wout(s, c, t)
                    if t == T - 1:
                        last.then_inc(chunk_used, 1)
                if t == 0:
                    last.then_inc(wout_done, 1)

            pe.wait_ge(small_in, 64)
            for b in range(4):
                t, c0 = b // 2, 4 * (b % 2)
                pe.wait_ge(h2n_ready, t + 1)
                for c in range(4):
                    last = nc.tensor.transpose(bank((0, 1, 4, 5)[b])[:, c * P:(c + 1) * P],
                                               h2n[:, t, (c0 + c) * P:(c0 + c + 1) * P], ident)
                last.then_inc(h2T_done, 1)
            for t in range(T):
                pe.wait_ge(h2T_ready, 2 * t + 2)
                lg = bank(3 + 4 * t)[:, 0:E]
                mm(lg, ones[0:1, 0:P], br[0:1, :], start=True, stop=False)
                for c in range(C):
                    last = mm(lg, h2T[:, t, c, :], wr[:, c, :], start=False, stop=(c == C - 1))
                last.then_inc(logits_done, 1)
            pe.wait_ge(member_ready, T)
            mm(bank(2)[:, 0:E], before, member[:, 0, :], start=True, stop=True)
            mm(bank(2)[:, E:2 * E], ones, member[:, 0, :], start=True, stop=False)
            mm(bank(2)[:, E:2 * E], before, member[:, 1, :], start=False, stop=True)
            mm(bank(2)[:, 2 * E:3 * E], ones, member[:, 0, :], start=True, stop=False)
            mm(bank(2)[:, 2 * E:3 * E], ones, member[:, 1, :], start=False, stop=True).then_inc(prefix_done, 1)
            for t in range(T):
                last = nc.tensor.transpose(bank(6)[0:E, t * P:(t + 1) * P], gates[:, t, 0:E], ident)
            last.then_inc(gatesT_done, 1)

            def put_transposes(m):
                pe.wait_ge(prep_ready, m + 1)
                pe.wait_ge(gh_ready, m)
                for t in range(T):
                    last = nc.tensor.transpose(bank(4)[:, t * P:(t + 1) * P], pickg[:, t, :], ident)
                last.then_inc(put_done, 1)

            def gather(m):
                pe.wait_ge(put_ready, m + 1)
                for c in range(C):
                    for t in range(T):
                        last = mm(bank(4)[:, c * SLOTS:(c + 1) * SLOTS], h2n[:, t, c * P:(c + 1) * P], pick[:, t, :],
                                  start=(t == 0), stop=(t == T - 1))
                last.then_inc(gather_done, 1)

            def expert_pe(n, m, i, u):
                put_transposes(m + 1)
                pe.wait_ge(gh_ready, m + 1)
                for v in range(2):
                    for half in range(2):
                        mm(bank(v)[64 * half:64 * half + 64, :], bsel[:, u % 2, :],
                           b1_sb[:, v * F + half * BANK:v * F + (half + 1) * BANK], start=True, stop=False)
                for k in range(W1_CHUNKS):
                    s, turn = slot_of(u, k)
                    pe.wait_ge(slot_full[s], i * (16 * TURNS) + 16 * (2 + turn))
                    for v in range(2):
                        for half in range(2):
                            last = mm(bank(v)[64 * half:64 * half + 64, :], gh[:, k, :],
                                      ring[:, s, v * F + half * BANK:v * F + (half + 1) * BANK],
                                      start=False, stop=(k == W1_CHUNKS - 1))
                    last.then_inc(chunk_used, 1)
                gather(m + 1)
                pe.wait_ge(act_ready, n + 1)
                for c in range(4):
                    last = nc.tensor.transpose(bank(5)[:, c * P:(c + 1) * P], a_sb[:, c * P:(c + 1) * P], ident)
                last.then_inc(actT_done, 1)
                pe.wait_ge(actT_ready, n + 1)
                for k in range(W2_CHUNKS):
                    s, turn = slot_of(u, W1_CHUNKS + k)
                    pe.wait_ge(slot_full[s], i * (16 * TURNS) + 16 * (2 + turn))
                    for c in (2 * k, 2 * k + 1):
                        for half in range(2):
                            last = mm(bank(5)[64 * half:64 * half + 64, :],
                                      aT[:, c % 4, 64 * (c // 4):64 * (c // 4) + 64],
                                      ring[:, s, (c % 2) * D + half * BANK:(c % 2) * D + (half + 1) * BANK],
                                      start=(c == 0), stop=(c == C - 1))
                    last.then_inc(chunk_used, 1)
                pe.wait_ge(y_ready, n + 1)
                for t in range(T):
                    for half in range(2):
                        r = slice(64 * half, 64 * half + 64)
                        last = mm(bank(2 + 4 * t + half), putb[r, u % 2, t * P:(t + 1) * P], y_sb[r, :],
                                  start=False, stop=False, skip_group_check=True)
                last.then_inc(combined, 1)

            pe.wait_ge(late_in, 48)
            pe.wait_ge(gatesT_ready, 1)
            pe.wait_ge(most_ready, 1)
            for t in range(T):
                for j in range(2):
                    mm(bank(2 + 4 * t + j), gatesT[:, t * P:(t + 1) * P], b2_sb[:, j * BANK:(j + 1) * BANK],
                       start=True, stop=False, skip_group_check=True)
            pe.wait_ge(prep_ready, 1)
            for t in range(T):
                last = nc.tensor.transpose(bank(4)[:, t * P:(t + 1) * P], pickg[:, t, :], ident)
            last.then_inc(put_done, 1)
            gather(0)
            with pe.Fori(0, ITERS) as i:
                for u in range(UNROLL):
                    expert_pe(i * UNROLL + u, i * UNROLL + u, i, u)
            most_v = pe.value_load(most_i[0:1, 0:1], min_val=0, max_val=SEQ)
            with pe.If(most_v > SLOTS):
                with pe.Fori(1, ROUNDS) as r:
                    put_transposes(r * (E + 1))
                    gather(r * (E + 1))
                    with pe.Fori(0, ITERS) as i:
                        for u in range(UNROLL):
                            expert_pe(r * E + i * UNROLL + u, r * (E + 1) + i * UNROLL + u, r * ITERS + i, u)


def constants():
    import numpy as np
    f = np.float32
    p = np.arange(P)
    col = {}
    col["ident"] = np.eye(P)
    col["before"] = p[:, None] < p[None, :]
    col["ones"] = np.ones((P, P))
    col["causal"] = np.where(p[None, :] <= p[:, None], 0.0, -1e30)
    log_g = np.log1p(-np.exp2(f(-5.0) - np.arange(RET_HEADS, dtype=f)))
    rel = (np.arange(SEQ)[None, :] - p[:, None]).astype(f)
    dec = np.where(rel >= 0, np.exp(log_g[:, None, None] * np.maximum(rel, 0)), 0) * f(RET_DK ** -0.5)
    col["decay"] = dec.transpose(1, 0, 2).reshape(P, -1)
    col["slot"] = np.tile(np.arange(SLOTS), (P, 2))
    col["expert"] = np.tile(np.arange(E), (P, 1))
    for name, dim, theta in (("ret", RET_DK, 10000.0), ("moba", MOBA_ROPE, 500000.0)):
        half = dim // 2
        inv = f(theta) ** (f(-2.0) * np.arange(half, dtype=f) / f(dim))
        ang = np.arange(SEQ, dtype=f)[:, None] * inv[None, :].astype(f)
        cos, sin = np.cos(ang), np.sin(ang)
        for part, tab in (("cos", np.concatenate([cos, cos], 1)), ("sin", np.concatenate([-sin, sin], 1))):
            col[f"{name}_{part}"] = tab.reshape(T, P, dim).transpose(1, 0, 2).reshape(P, -1)
    return np.concatenate([col[n].astype(f) for n, _ in CONST_PARTS], axis=1)


_INS = ["x", "norm1_w", "w_in", "ret_norm_w", "w_out", "norm2_w", "w_router", "b_router",
        "w1", "b1", "w2", "b2", "final_norm_w"]


def kernel(**inputs):
    import numpy as np
    import concourse.bacc as bacc
    from concourse.bass_utils import run_bass_kernel_spmd

    nc = bacc.Bacc("TRN2", target_bir_lowering=False, num_devices=1)
    arrays, args = {}, []
    for name, a in [(n, inputs[n]) for n in _INS] + [("consts", constants())]:
        a = np.ascontiguousarray(a)
        arrays[f"in_{name}"] = a
        args.append(nc.dram_tensor(f"in_{name}", a.shape, mybir.dt.from_np(a.dtype), kind="ExternalInput").ap())
    args.append(nc.dram_tensor("out_0", (1, SEQ, D), F32, kind="ExternalOutput").ap())
    layer_kernel(nc, *args)
    r = run_bass_kernel_spmd(nc, [arrays], core_ids=[0])
    return r.results[0]["out_0"]
```

```python
import concourse.bass as bass
from concourse import mybir
from contextlib import ExitStack

F32 = mybir.dt.float32
BF16 = mybir.dt.bfloat16
I32 = mybir.dt.int32
ALU = mybir.AluOpType
ACT = mybir.ActivationFunctionType
AX = mybir.AxisListType

P = 128
SEQ = 256
T = SEQ // P
D = 1024
C = D // P
RET_HEADS, RET_DK, RET_DV = 4, 64, 128
MOBA_HEADS, MOBA_DH, MOBA_ROPE = 8, 64, 16
D_IN = 3072
E = 32
TOPK = 4
F = 1024
SLOTS = 64
ROUNDS = SEQ // SLOTS
BANK = 512
LIMIT, ALPHA = 7.0, 1.702
RMS_EPS, GN_EPS = 1e-5, 1e-6

RING = 20
SLOT_COLS = 2048
WIN_COLS = SLOT_COLS // C
WIN_CHUNKS = D_IN // WIN_COLS
WOUT_CHUNKS = C // 2
HEAD_CHUNKS = WIN_CHUNKS + WOUT_CHUNKS
W1_CHUNKS = C
W2_CHUNKS = C // 2
EXPERT_CHUNKS = W1_CHUNKS + W2_CHUNKS
ROUND_CHUNKS = E * EXPERT_CHUNKS
PEEL = 2
UNROLL = 5
ITERS = (E - PEEL) // UNROLL
TURNS = UNROLL * EXPERT_CHUNKS // RING
assert PEEL + ITERS * UNROLL == E and TURNS * RING == UNROLL * EXPERT_CHUNKS
SENTINEL = 3.0e38

RQ, RK, RV, RG, MQ, MK, MV = 0, 256, 512, 1024, 1536, 2048, 2560
CHUNK_COL = [MQ, MK, MQ + 256, MK + 256, MV, MV + 256, RQ, RK, RV, RV + 256, RG, RG + 256]
FIRST_ORDER = list(range(14)) + [16, 17, 18, 14, 15, 19]
WOUT_ORDER = [2, 3, 0, 1]

CONST_PARTS = [("ident", P), ("before", P), ("ones", P), ("causal", P), ("decay", RET_HEADS * SEQ),
               ("slot", 2 * SLOTS), ("row", E + 1), ("ret_cos", T * RET_DK), ("ret_sin", T * RET_DK),
               ("moba_cos", T * MOBA_ROPE), ("moba_sin", T * MOBA_ROPE)]
CONST_COLS = sum(n for _, n in CONST_PARTS)


def col(e):
    return slice(e, e + 1) if isinstance(e, int) else bass.ds(e, 1)


def local_expert(i, j):
    return i * UNROLL + j


def slot_of(j, k):
    return (j * EXPERT_CHUNKS + k) % RING


def slot_count(r, i, j, k):
    s, g = slot_of(j, k), j * EXPERT_CHUNKS + k
    head = 1 if s < HEAD_CHUNKS else 0
    per_round = len(range(s, ROUND_CHUNKS, RING))
    return 16 * (r * per_round + i * TURNS + (head + g // RING + 1))


def layer_kernel(nc, x, norm1_w, w_in, ret_norm_w, w_out, norm2_w, w_router, b_router,
                 w1, b1, w2, b2, final_norm_w, consts, out):
    x_v = x.rearrange("b (t p) d -> p (b t) d", p=P)
    out_v = out.rearrange("b (t p) d -> p (b t) d", p=P)
    win_v = w_in.rearrange("l (c p) n -> p (l c) n", p=P)
    wout_v = w_out.rearrange("l (c p) n -> p (l c) n", p=P)
    w1_v = w1.rearrange("l e (c p) n -> (l e) c p n", p=P)
    w2_v = w2.rearrange("l e (c p) n -> (l e) p c n", p=P)

    ctx = ExitStack()
    with ctx:
        def sb(name, shape, dt=F32):
            return ctx.enter_context(nc.sbuf_tensor(name, shape, dt))

        def sem(name):
            return ctx.enter_context(nc.semaphore(name))

        ctx.enter_context(nc.allow_non_contiguous_dma(reason="norm weights, one element per partition and tile"))
        PS = ctx.enter_context(nc.psum_tensor("PS", [P, 8 * BANK], F32))

        def bank(b, n=1):
            return PS[:, b * BANK:(b + n) * BANK]

        ring = sb("ring", [P, RING, SLOT_COLS])
        cst = sb("cst", [P, CONST_COLS])
        resid = sb("resid", [P, T, D])
        hT = sb("hT", [P, T, C, P])
        work = sb("work", [P, 12 * SEQ + 4 * 3 * P])
        nat_flat = ring[:, HEAD_CHUNKS:HEAD_CHUNKS + 3, :].rearrange("p s n -> p (s n)")
        nat = nat_flat.rearrange("p (t n) -> p t n", t=T)
        mixT = ring[:, HEAD_CHUNKS + 3, :].rearrange("p (c n) -> p c n", c=C)
        n1w = sb("n1w", [P, C])
        n2w = sb("n2w", [P, C])
        brb = sb("brb", [P, E])
        wr = sb("wr", [P, C, E])
        stat = sb("stat", [P, 64])
        bn = sb("bn", [P, T * RET_HEADS, 6])
        gn = sb("gn", [P, T * RET_HEADS, 2])
        gn_rstd = sb("gn_rstd", [P, T * RET_HEADS])
        logits = sb("logits", [P, T, E + TOPK])
        marked = sb("marked", [P, T, E + TOPK])
        expl = sb("expl", [P, T, E])
        top = sb("top", [P, T, 8])
        gates = sb("gates", [P, T, E + 1])
        member = sb("member", [P, T, E], BF16)
        count_w = sb("count_w", [P, 2 * P], BF16)
        place = sb("place", [P, T, E + 1])
        most = sb("most", [P, 1])
        most_i = sb("most_i", [1, 1], I32)

        c_at, at = {}, 0
        for name, n in CONST_PARTS:
            c_at[name] = cst[:, at:at + n]
            at += n
        ident, before, ones, causal = (c_at[n] for n in ("ident", "before", "ones", "causal"))
        decay = c_at["decay"].rearrange("p (h n) -> p h n", h=RET_HEADS)
        slot_id = c_at["slot"]
        row_id = c_at["row"]
        ret_cos = c_at["ret_cos"].rearrange("p (t d) -> p t d", t=T)
        ret_sin = c_at["ret_sin"].rearrange("p (t d) -> p t d", t=T)
        moba_cos = c_at["moba_cos"].rearrange("p (t d) -> p t d", t=T)
        moba_sin = c_at["moba_sin"].rearrange("p (t d) -> p t d", t=T)

        qkT = work[:, 0:12 * SEQ].rearrange("p (i n) -> p i n", n=SEQ)
        prob = work[:, 3072:3840].rearrange("p (s n) -> p s n", s=2)
        probT = work[:, 3840:4608].rearrange("p (s n) -> p s n", s=2)
        decayed = prob
        retw = nat[:, 0, MQ:MQ + 512]
        ret = nat[:, :, RQ:RQ + 512]

        h2T = work[:, 0:2048].rearrange("p (t c n) -> p t c n", t=T, c=C)
        b1_sb = hT[0:2 * E, 0, :, :].rearrange("p c n -> p (c n)")
        b2_sb = work[0:E, 3584:4608]
        dump = hT[:, 1, :, :].rearrange("p c n -> p (c n)")
        fnw_slot = ROUND_CHUNKS % RING
        fnw = ring[:, fnw_slot, 0:D]
        gh = work[:, 0:512].rearrange("p (c s) -> p c s", c=C)
        pick = work[:, 512:640].rearrange("p (t s) -> p t s", t=T)
        pickg = work[:, 640:896].rearrange("p (t s) -> p t s", t=T)
        putb = work[:, 896:1152]
        bsel = work[0:2 * E, 1408:1472]
        g_sb = work[:, 1536:2048]
        l_sb = work[:, 2048:2560]
        s_sb = work[:, 2560:3072]
        a_sb = work[:, 3072:3584]
        aT = work[:, 3584:4096].rearrange("p (c n) -> p c n", c=4)
        y_sb = work[:, 4096:4608]

        scr = sb("scr", [P, 256])
        gsig = nat[:, :, MK:MK + 512]
        gatesT = scr[0:E, 0:SEQ]

        slot_full = [sem(f"slot_full{s}") for s in range(RING)]
        chunk_used = sem("chunk_used")
        x_in = [sem(f"x_in{t}") for t in range(T)]
        cst_in = sem("cst_in")
        ident_in = sem("ident_in")
        n1w_in = sem("n1w_in")
        small_in = sem("small_in")
        fnw_in = sem("fnw_in")
        warm = sem("warm")
        retw_in = sem("retw_in")
        late_in = sem("late_in")
        out_done = sem("out_done")
        sumsq_ready = sem("sumsq_ready")
        var_ready = sem("var_ready")
        std_ready = sem("std_ready")
        rstd_ready = sem("rstd_ready")
        xT_done = sem("xT_done")
        hT_ready = sem("hT_ready")
        nat_ready = sem("nat_ready")
        roped = sem("roped")
        qkT_done = sem("qkT_done")
        qkT_ready = sem("qkT_ready")
        score_done = sem("score_done")
        masked = sem("masked")
        negmax_ready = sem("negmax_ready")
        exp_ready = sem("exp_ready")
        prob_ready = sem("prob_ready")
        probT_done = sem("probT_done")
        probT_ready = sem("probT_ready")
        pv_done = sem("pv_done")
        pv_taken = sem("pv_taken")
        rscore_done = sem("rscore_done")
        decayed_ready = sem("decayed_ready")
        ret_done = sem("ret_done")
        siglu_ready = sem("siglu_ready")
        gnvar_ready = sem("gnvar_ready")
        gnstd_ready = sem("gnstd_ready")
        ret_ready = sem("ret_ready")
        retT_done = sem("retT_done")
        retT_ready = sem("retT_ready")
        wout_done = sem("wout_done")
        x2_ready = sem("x2_ready")
        h2T_done = sem("h2T_done")
        h2T_ready = sem("h2T_ready")
        logits_done = sem("logits_done")
        top_ready = sem("top_ready")
        topexp_ready = sem("topexp_ready")
        member_ready = sem("member_ready")
        prefix_done = sem("prefix_done")
        gatesT_done = sem("gatesT_done")
        gatesT_ready = sem("gatesT_ready")
        place_ready = sem("place_ready")
        most_ready = sem("most_ready")
        dve_step = sem("dve_step")
        pick_ready = sem("pick_ready")
        pickg_ready = sem("pickg_ready")
        put_done = sem("put_done")
        put_ready = sem("put_ready")
        gather_done = sem("gather_done")
        gh_ready = sem("gh_ready")
        gate_ready = sem("gate_ready")
        lin_ready = sem("lin_ready")
        glin_ready = sem("glin_ready")
        sig_ready = sem("sig_ready")
        act_ready = sem("act_ready")
        actT_done = sem("actT_done")
        actT_ready = sem("actT_ready")
        y_ready = sem("y_ready")
        combined = sem("combined")
        final_ready = sem("final_ready")
        outrow_ready = sem("outrow_ready")

        def run_experts(eng, expert, r):
            for j in range(PEEL):
                expert(r, 0, j)
            with eng.Fori(0, ITERS) as i:
                for j in range(PEEL, PEEL + UNROLL):
                    expert(r, i, j)

        def up_done(n):
            return n * EXPERT_CHUNKS + (HEAD_CHUNKS + W1_CHUNKS)

        def down_done(n):
            return n * EXPERT_CHUNKS + (HEAD_CHUNKS + EXPERT_CHUNKS)

        block = ctx.enter_context(nc.Block())

        @block.sync
        def _(sp):
            for t in range(T):
                sp.dma_start(resid[:, t, :], x_v[:, t, :]).then_inc(x_in[t], 16)
            for j, col in enumerate(CHUNK_COL):
                dst = ring[:, j, :].rearrange("p (c n) -> p c n", c=C)
                sp.dma_start(dst, win_v[:, :, col:col + WIN_COLS]).then_inc(slot_full[j], 16)
            for j, pair in enumerate(WOUT_ORDER):
                s = WIN_CHUNKS + j
                dst = ring[:, s, :].rearrange("p (c n) -> p c n", c=2)
                sp.dma_start(dst, wout_v[:, 2 * pair:2 * pair + 2, :]).then_inc(slot_full[s], 16)

            def load(r, i, j, k):
                e, s = local_expert(i, j), slot_of(j, k)
                if k < W1_CHUNKS:
                    sp.dma_start(ring[:, s, :], w1_v[e, k, :, :]).then_inc(slot_full[s], 16)
                else:
                    c = 2 * (k - W1_CHUNKS)
                    dst = ring[:, s, :].rearrange("p (c n) -> p c n", c=2)
                    sp.dma_start(dst, w2_v[e, :, c:c + 2, :]).then_inc(slot_full[s], 16)

            for g in FIRST_ORDER:
                if g < HEAD_CHUNKS:
                    sp.wait_ge(chunk_used, g + 1)
                elif g < HEAD_CHUNKS + 3:
                    sp.wait_ge(retT_done, 2)
                else:
                    sp.wait_ge(chunk_used, HEAD_CHUNKS)
                load(0, 0, g // EXPERT_CHUNKS, g % EXPERT_CHUNKS)

            def expert_loads(r, i, j):
                for k in range(EXPERT_CHUNKS):
                    g = j * EXPERT_CHUNKS + k
                    if j < PEEL and g < RING:
                        if isinstance(r, int):
                            continue
                        sp.wait_ge(chunk_used, r * ROUND_CHUNKS + HEAD_CHUNKS)
                    else:
                        sp.wait_ge(chunk_used, r * ROUND_CHUNKS + i * (UNROLL * EXPERT_CHUNKS)
                                   + (HEAD_CHUNKS + g - RING + 1))
                    load(r, i, j, k)

            run_experts(sp, expert_loads, 0)
            sp.wait_ge(most_ready, 1)
            most_v = sp.value_load(most_i[0:1, 0:1], min_val=0, max_val=SEQ)
            with sp.If(most_v > SLOTS):
                with sp.Fori(1, ROUNDS) as r:
                    run_experts(sp, expert_loads, r)
                sp.wait_ge(chunk_used, ROUNDS * ROUND_CHUNKS + HEAD_CHUNKS)
            sp.wait_ge(chunk_used, ROUND_CHUNKS + HEAD_CHUNKS - RING + 1)
            sp.dma_start(fnw, final_norm_w.rearrange("(a n) -> a n", a=1).broadcast_to([P, D])).then_inc(fnw_in, 16)
            for t in range(T):
                sp.wait_ge(outrow_ready, t + 1)
                sp.dma_start(out_v[:, t, :], resid[:, t, :]).then_inc(out_done, 16)
            sp.wait_ge(out_done, 16 * T)

        @block.gpsimd
        def _(pool):
            pool.wait_ge(qkT_done, 4)
            pool.dma_start(retw, ret_norm_w.broadcast_to([P, 512])).then_inc(retw_in, 16)
            pool.wait_ge(chunk_used, WIN_CHUNKS)
            for v in range(2):
                pool.dma_start(b1_sb[v * E:(v + 1) * E, :], b1[0, :, v * F:(v + 1) * F]).then_inc(late_in, 16)
            pool.wait_ge(probT_ready, MOBA_HEADS)
            pool.wait_ge(ret_done, RET_HEADS)
            pool.wait_ge(pv_done, 4)
            pool.dma_start(b2_sb, b2[0, :, :]).then_inc(late_in, 16)
            pool.wait_ge(late_in, 48)

        @block.scalar
        def _(act):
            act.dma_start(ident, consts[:, 0:P]).then_inc(ident_in, 16)
            act.dma_start(n1w[:, :], norm1_w.rearrange("l (c p) -> p (l c)", p=P)).then_inc(n1w_in, 16)
            act.dma_start(cst[:, P:], consts[:, P:]).then_inc(cst_in, 16)
            act.dma_start(n2w[:, :], norm2_w.rearrange("l (c p) -> p (l c)", p=P)).then_inc(small_in, 16)
            act.dma_start(brb[:, :], b_router.broadcast_to([P, E])).then_inc(small_in, 16)
            act.dma_start(wr[:, :, :], w_router.rearrange("l (c p) n -> p (l c) n", p=P)).then_inc(small_in, 16)

            act.wait_ge(warm, 1)
            nc.scalar.activation(stat[:, 63:64], stat[:, 62:63], ACT.Sqrt)
            for t in range(T):
                act.wait_ge(x_in[t], 16)
                if t:
                    act.wait_ge(sumsq_ready, t)
                nc.scalar.activation(work[:, 0:D], resid[:, t, :], ACT.Square, scale=1.0 / 32.0,
                                     accum_out=stat[:, t:t + 1]).then_inc(sumsq_ready, 1)
            act.wait_ge(var_ready, 1)
            nc.scalar.activation(stat[:, 4:6], stat[:, 2:4], ACT.Sqrt).then_inc(std_ready, 1)

            def take_proj(j):
                act.wait_ge(chunk_used, j + 1)
                c0 = CHUNK_COL[j]
                for t in range(T):
                    ins = nc.scalar.activation(nat[:, t, c0:c0 + WIN_COLS],
                                               bank(4 + j % 2)[:, t * WIN_COLS:(t + 1) * WIN_COLS], ACT.Copy,
                                               scale=stat[:, 6 + t:7 + t])
                ins.then_inc(nat_ready, 1)

            def exps(g):
                for h in (2 * g, 2 * g + 1):
                    act.wait_ge(negmax_ready, h + 1)
                    for t, (a, b) in enumerate(((0, P), (P, 3 * P))):
                        nc.scalar.activation(prob[:, h % 2, a:b], prob[:, h % 2, a:b], ACT.Exp,
                                             bias=stat[:, 8 + 2 * (h % 2) + t:9 + 2 * (h % 2) + t],
                                             scale=MOBA_DH ** -0.5,
                                             accum_out=stat[:, 12 + 2 * (h % 2) + t:13 + 2 * (h % 2) + t]
                                             ).then_inc(exp_ready, 1)

            act.wait_ge(rstd_ready, 1)
            for j in range(6):
                take_proj(j)
            exps(0)
            take_proj(6)
            exps(1)
            take_proj(7)
            exps(2)
            take_proj(8)
            exps(3)
            take_proj(9)
            take_proj(10)
            take_proj(11)
            act.wait_ge(nat_ready, WIN_CHUNKS)
            for t in range(T):
                nc.scalar.activation(gsig[:, t, :], nat[:, t, RG:RG + 512], ACT.Sigmoid).then_inc(siglu_ready, 1)
            act.wait_ge(gnvar_ready, 1)
            nc.scalar.activation(gn_rstd[:, :], gn_rstd[:, :], ACT.Sqrt).then_inc(gnstd_ready, 1)
            for t in range(T):
                act.wait_ge(x2_ready, t + 1)
                act.wait_ge(sumsq_ready, T + t)
                nc.scalar.activation(dump, resid[:, t, :], ACT.Square, scale=1.0 / 32.0,
                                     accum_out=stat[:, t:t + 1]).then_inc(sumsq_ready, 1)
                act.wait_ge(var_ready, 2 + t)
                nc.scalar.activation(stat[:, 4 + t:5 + t], stat[:, 2 + t:3 + t], ACT.Sqrt).then_inc(std_ready, 1)
            for t in range(T):
                act.wait_ge(top_ready, t + 1)
                nc.scalar.activation(expl[:, t, :], logits[:, t, 0:E], ACT.Exp,
                                     bias=stat[:, 20 + t:21 + t]).then_inc(topexp_ready, 1)

            def expert_act(r, i, j):
                n = r * E + local_expert(i, j)
                act.wait_ge(gate_ready, n + 1)
                nc.scalar.activation(s_sb, g_sb, ACT.Sigmoid, scale=ALPHA).then_inc(sig_ready, 1)
                act.wait_ge(actT_done, n + 1)
                nc.scalar.activation(aT, bank(5).rearrange("p (c n) -> p c n", c=4), ACT.Copy).then_inc(actT_ready, 1)
                act.wait_ge(chunk_used, down_done(n))
                nc.scalar.activation(y_sb, bank(5), ACT.Copy).then_inc(y_ready, 1)

            run_experts(act, expert_act, 0)
            act.wait_ge(most_ready, 1)
            most_v = act.value_load(most_i[0:1, 0:1], min_val=0, max_val=SEQ)
            with act.If(most_v > SLOTS):
                with act.Fori(1, ROUNDS) as r:
                    run_experts(act, expert_act, r)
            nc.scalar.activation(stat[:, 61:62], stat[:, 62:63], ACT.Sqrt)
            for t in range(T):
                act.wait_ge(final_ready, t + 1)
                act.wait_ge(sumsq_ready, 2 * T + t)
                nc.scalar.activation(dump, resid[:, t, :], ACT.Square, scale=1.0 / 32.0,
                                     accum_out=stat[:, t:t + 1]).then_inc(sumsq_ready, 1)
                act.wait_ge(var_ready, 4 + t)
                nc.scalar.activation(stat[:, 4 + t:5 + t], stat[:, 2 + t:3 + t], ACT.Sqrt).then_inc(std_ready, 1)

        @block.vector
        def _(dve):
            steps = [0]

            def link(ins):
                steps[0] += 1
                ins.then_inc(dve_step, 1)
                dve.wait_ge(dve_step, steps[0])

            nc.vector.memset(stat[:, 62:63], 1.0).then_inc(warm, 1)
            nc.vector.memset(gates[:, :, :], 0.0)
            nc.vector.memset(logits[:, :, :], -SENTINEL)
            link(nc.vector.memset(place[:, :, :], -1.0))

            def w_cols(w, c0):
                return w[:, c0:c0 + 4].unsqueeze(2).broadcast_to([P, 4, P])

            dve.wait_ge(n1w_in, 16)
            for b in range(4):
                t, c0 = b // 2, 4 * (b % 2)
                dve.wait_ge(xT_done, b + 1)
                nc.vector.tensor_tensor(hT[:, t, c0:c0 + 4, :], bank(b).rearrange("p (c n) -> p c n", c=4),
                                        w_cols(n1w, c0), ALU.mult).then_inc(hT_ready, 1)
            dve.wait_ge(sumsq_ready, T)
            nc.vector.tensor_scalar(stat[:, 2:4], stat[:, 0:2], RMS_EPS, None, ALU.add).then_inc(var_ready, 1)
            dve.wait_ge(std_ready, 1)
            nc.vector.reciprocal(stat[:, 6:8], stat[:, 4:6]).then_inc(rstd_ready, 1)
            dve.wait_ge(cst_in, 16)
            nc.vector.tensor_copy(count_w[:, :], cst[:, P:3 * P])

            rotations = [0]

            def rope(j):
                dve.wait_ge(nat_ready, j + 1)
                if rotations[0]:
                    dve.wait_ge(roped, rotations[0])
                rotations[0] += 1
                retention = CHUNK_COL[j] in (RQ, RK)
                dim = RET_DK if retention else MOBA_ROPE
                cos, sin = (ret_cos, ret_sin) if retention else (moba_cos, moba_sin)
                half, heads = dim // 2, WIN_COLS // 64
                for t in range(T):
                    v = nat[:, t, CHUNK_COL[j]:CHUNK_COL[j] + WIN_COLS].rearrange("p (h d) -> p h d", h=heads)
                    swapped = scr[:, 0:heads * dim].rearrange("p (h d) -> p h d", h=heads)

                    def table(tab, a, b):
                        return tab[:, t, a:b].unsqueeze(1).broadcast_to([P, heads, b - a])

                    nc.vector.tensor_tensor(swapped[:, :, 0:half], v[:, :, half:dim], table(sin, 0, half), ALU.mult)
                    link(nc.vector.tensor_tensor(swapped[:, :, half:dim], v[:, :, 0:half], table(sin, half, dim),
                                                 ALU.mult))
                    link(nc.vector.tensor_tensor(v[:, :, 0:dim], v[:, :, 0:dim], table(cos, 0, dim), ALU.mult))
                    ins = nc.vector.tensor_tensor(v[:, :, 0:dim], v[:, :, 0:dim], swapped, ALU.add)
                    if t == 0:
                        link(ins)
                ins.then_inc(roped, 1)

            def take_qkT(i, tile):
                dve.wait_ge(qkT_done, i + 1)
                nc.vector.tensor_copy(qkT[:, tile:tile + 2, :],
                                      bank(6).rearrange("p (i n) -> p i n", i=2)).then_inc(qkT_ready, 1)

            def mask_max(g):
                for h in (2 * g, 2 * g + 1):
                    s = bank(h % 2)
                    diag = s[:, 0:3 * P].rearrange("p (b n) -> p b n", b=3)[:, 0:3:2, :]
                    pdiag = prob[:, h % 2, :].rearrange("p (b n) -> p b n", b=3)[:, 0:3:2, :]
                    dve.wait_ge(score_done, h + 1)
                    nc.vector.tensor_tensor(pdiag, diag, causal.unsqueeze(1).broadcast_to([P, 2, P]), ALU.add)
                    nc.vector.tensor_copy(prob[:, h % 2, P:2 * P], s[:, P:2 * P]).then_inc(masked, 1)
                    dve.wait_ge(masked, h + 1)
                    if h >= 2:
                        dve.wait_ge(negmax_ready, h - 1)
                    m = stat[:, 16 + 2 * (h % 2):18 + 2 * (h % 2)]
                    nc.vector.reduce_max(m[:, 0:1], prob[:, h % 2, 0:P], AX.X)
                    link(nc.vector.reduce_max(m[:, 1:2], prob[:, h % 2, P:3 * P], AX.X))
                    nc.vector.tensor_scalar(stat[:, 8 + 2 * (h % 2):10 + 2 * (h % 2)], m, -MOBA_DH ** -0.5, None,
                                            ALU.mult).then_inc(negmax_ready, 1)

            def normalise(g):
                for h in (2 * g, 2 * g + 1):
                    dve.wait_ge(exp_ready, 2 * h + 2)
                    if h >= 2:
                        dve.wait_ge(prob_ready, h - 1)
                    r = stat[:, 28 + 2 * (h % 2):30 + 2 * (h % 2)]
                    link(nc.vector.reciprocal(r, stat[:, 12 + 2 * (h % 2):14 + 2 * (h % 2)]))
                    nc.vector.tensor_scalar(prob[:, h % 2, 0:P], prob[:, h % 2, 0:P], r[:, 0:1], None, ALU.mult)
                    nc.vector.tensor_scalar(prob[:, h % 2, P:3 * P], prob[:, h % 2, P:3 * P], r[:, 1:2], None,
                                            ALU.mult).then_inc(prob_ready, 1)

            def take_probT(g):
                for h in (2 * g, 2 * g + 1):
                    dve.wait_ge(probT_done, h + 1)
                    nc.vector.tensor_copy(probT[:, h % 2, :], bank(2 if h % 2 == 0 else 7)[:, 0:3 * P]
                                          ).then_inc(probT_ready, 1)

            def take_pv(g):
                dve.wait_ge(pv_done, g + 1)
                nc.vector.tensor_copy(mixT[:, 4 + g, :], bank(3)[:, 0:SEQ]).then_inc(pv_taken, 1)

            rope(0)
            rope(1)
            take_qkT(0, 4)
            rope(2)
            take_qkT(1, 8)
            rope(3)
            take_qkT(2, 6)
            take_qkT(3, 10)
            mask_max(0)
            normalise(0)
            take_probT(0)
            mask_max(1)
            normalise(1)
            rope(6)
            take_qkT(4, 0)
            take_pv(0)
            take_probT(1)
            mask_max(2)
            normalise(2)
            rope(7)
            take_qkT(5, 2)
            take_pv(1)
            take_probT(2)
            mask_max(3)
            normalise(3)
            take_pv(2)
            take_probT(3)
            take_pv(3)
            for h in range(RET_HEADS):
                dve.wait_ge(rscore_done, h + 1)
                if h >= 2:
                    dve.wait_ge(ret_done, h - 1)
                s = bank(6 + h % 2)
                nc.vector.tensor_tensor(decayed[:, h % 2, 0:SEQ], s[:, 0:SEQ], decay[:, h, :], ALU.mult)
                nc.vector.tensor_tensor(decayed[:, h % 2, SEQ:SEQ + P], s[:, SEQ:SEQ + P], decay[:, h, 0:P],
                                        ALU.mult).then_inc(decayed_ready, 1)
            dve.wait_ge(retw_in, 16)
            dve.wait_ge(nat_ready, WIN_CHUNKS)
            dve.wait_ge(siglu_ready, T)
            for t in range(T):
                link(nc.vector.tensor_tensor(nat[:, t, RG:RG + 512], nat[:, t, RG:RG + 512], gsig[:, t, :], ALU.mult))
                link(nc.vector.tensor_tensor(nat[:, t, RG:RG + 512], nat[:, t, RG:RG + 512], retw, ALU.mult))
            dve.wait_ge(ret_done, RET_HEADS)
            for t in range(T):
                for h in range(RET_HEADS):
                    nc_in = bank(t)[:, h * RET_DV:(h + 1) * RET_DV]
                    ins = nc.vector.bn_stats(bn[:, t * RET_HEADS + h, :], nc_in)
            link(ins)
            for g in range(T * RET_HEADS):
                ins = nc.vector.bn_aggr(gn[:, g, :], bn[:, g, :])
            link(ins)
            nc.vector.tensor_scalar(gn_rstd[:, :], gn[:, :, 1], GN_EPS, None, ALU.add).then_inc(gnvar_ready, 1)
            dve.wait_ge(gnstd_ready, 1)
            link(nc.vector.reciprocal(gn_rstd[:, :], gn_rstd[:, :]))
            for t in range(T):
                for h in range(RET_HEADS):
                    g = t * RET_HEADS + h
                    ins = nc.vector.tensor_scalar(ret[:, t, h * RET_DV:(h + 1) * RET_DV],
                                                  bank(t)[:, h * RET_DV:(h + 1) * RET_DV],
                                                  gn[:, g, 0:1], gn_rstd[:, g:g + 1], ALU.subtract, ALU.mult)
                link(ins)
                nc.vector.tensor_tensor(ret[:, t, :], ret[:, t, :], nat[:, t, RG:RG + 512],
                                        ALU.mult).then_inc(ret_ready, 1)
            for i in range(2):
                dve.wait_ge(retT_done, i + 1)
                nc.vector.tensor_copy(mixT[:, 2 * i:2 * i + 2, :],
                                      bank(4 + i).rearrange("p (i n) -> p i n", i=2)).then_inc(retT_ready, 1)
            dve.wait_ge(small_in, 48)
            for t in range(T):
                if t == 0:
                    dve.wait_ge(wout_done, 1)
                else:
                    dve.wait_ge(chunk_used, HEAD_CHUNKS)
                nc.vector.tensor_tensor(resid[:, t, :], resid[:, t, :], bank(2 + 4 * t, 2), ALU.add).then_inc(x2_ready, 1)
                for b in (2 * t, 2 * t + 1):
                    c0 = 4 * (b % 2)
                    dve.wait_ge(h2T_done, b + 1)
                    nc.vector.tensor_tensor(h2T[:, t, c0:c0 + 4, :],
                                            bank((0, 1, 4, 5)[b]).rearrange("p (c n) -> p c n", c=4),
                                            w_cols(n2w, c0), ALU.mult).then_inc(h2T_ready, 1)
                dve.wait_ge(sumsq_ready, T + t + 1)
                nc.vector.tensor_scalar(stat[:, 2 + t:3 + t], stat[:, t:t + 1], RMS_EPS, None,
                                        ALU.add).then_inc(var_ready, 1)
                dve.wait_ge(std_ready, 2 + t)
                link(nc.vector.reciprocal(stat[:, 6 + t:7 + t], stat[:, 4 + t:5 + t]))
            for t in range(T):
                dve.wait_ge(logits_done, t + 1)
                link(nc.vector.scalar_tensor_tensor(logits[:, t, 0:E], bank(3 + 4 * t)[:, 0:E], stat[:, 6 + t:7 + t],
                                                    brb[:, :], ALU.mult, ALU.add))
                link(nc.vector.max(top[:, t, :], logits[:, t, 0:E]))
                nc.vector.tensor_scalar(stat[:, 20 + t:21 + t], top[:, t, 0:1], -1.0, None,
                                        ALU.mult).then_inc(top_ready, 1)
                link(nc.vector.memset(top[:, t, TOPK:8], -SENTINEL))
                link(nc.vector.match_replace(marked[:, t, :], top[:, t, :], logits[:, t, :], SENTINEL))
                nc.vector.tensor_scalar(member[:, t, :], marked[:, t, 0:E], SENTINEL, None,
                                        ALU.is_equal).then_inc(member_ready, 1)
            dve.wait_ge(member_ready, T)
            dve.wait_ge(prefix_done, 1)
            link(nc.vector.scalar_tensor_tensor(place[:, :, 0:E], bank(2)[:, 0:T * E].rearrange("p (t e) -> p t e", t=T),
                                                1.0, member[:, :, :], ALU.add, ALU.mult))
            link(nc.vector.tensor_scalar(place[:, :, 0:E], place[:, :, 0:E], -1.0, None, ALU.add))

            def make_pick(e):
                for t in range(T):
                    ins = nc.vector.tensor_scalar(pick[:, t, :], slot_id[:, 0:SLOTS], place[:, t, col(e)],
                                                  stat[:, 6 + t:7 + t], ALU.is_equal, ALU.mult)
                ins.then_inc(pick_ready, 1)

            def make_pickg(e):
                for t in range(T):
                    ins = nc.vector.tensor_scalar(pickg[:, t, :], slot_id, place[:, t, col(e)], gates[:, t, col(e)],
                                                  ALU.is_equal, ALU.mult)
                ins.then_inc(pickg_ready, 1)

            make_pick(0)
            for t in range(T):
                dve.wait_ge(topexp_ready, t + 1)
                link(nc.vector.scalar_tensor_tensor(gates[:, t, 0:E], marked[:, t, 0:E], SENTINEL, expl[:, t, :],
                                                    ALU.is_equal, ALU.mult))
                link(nc.vector.reduce_sum(stat[:, 24 + t:25 + t], gates[:, t, 0:E], AX.X))
                link(nc.vector.reciprocal(stat[:, 26 + t:27 + t], stat[:, 24 + t:25 + t]))
                link(nc.vector.tensor_scalar(gates[:, t, 0:E], gates[:, t, 0:E], stat[:, 26 + t:27 + t], None, ALU.mult))
            make_pickg(0)
            link(nc.vector.reduce_max(most[:, :], bank(2)[:, T * E:(T + 1) * E], AX.X))
            nc.vector.tensor_copy(most_i[:, :], most[0:1, :]).then_inc(most_ready, 1)

            def make_bsel(e):
                nc.vector.tensor_copy(bsel, row_id[0:2 * E, col(e)].broadcast_to([2 * E, SLOTS]))

            def take_gather(m):
                dve.wait_ge(gather_done, m + 1)
                nc.vector.tensor_tensor(gh, bank(4).rearrange("p (c s) -> p c s", c=C),
                                        n2w[:, :].unsqueeze(2).broadcast_to([P, C, SLOTS]), ALU.mult
                                        ).then_inc(gh_ready, 1)

            def expert_dve(r, i, j):
                e = local_expert(i, j)
                n, m = r * E + e, r * (E + 1) + e
                dve.wait_ge(put_done, n + 1)
                nc.vector.tensor_copy(putb, bank(4)[:, 0:SEQ]).then_inc(put_ready, 1)
                dve.wait_ge(gather_done, m + 1)
                make_pick(e + 1)
                make_pickg(e + 1)
                dve.wait_ge(chunk_used, up_done(n))
                nc.vector.tensor_scalar(g_sb, bank(0), LIMIT, None, ALU.min).then_inc(gate_ready, 1)
                nc.vector.tensor_scalar(l_sb, bank(1), LIMIT, -LIMIT, ALU.min, ALU.max).then_inc(lin_ready, 1)
                dve.wait_ge(gate_ready, n + 1)
                dve.wait_ge(lin_ready, n + 1)
                nc.vector.scalar_tensor_tensor(l_sb, l_sb, 1.0, g_sb, ALU.add, ALU.mult).then_inc(glin_ready, 1)
                dve.wait_ge(glin_ready, n + 1)
                dve.wait_ge(sig_ready, n + 1)
                nc.vector.tensor_tensor(a_sb, l_sb, s_sb, ALU.mult).then_inc(act_ready, 1)
                make_bsel(e + 1)
                take_gather(m + 1)

            make_bsel(0)
            take_gather(0)
            dve.wait_ge(gatesT_done, 1)
            nc.vector.tensor_copy(gatesT, bank(5)[0:E, 0:SEQ]).then_inc(gatesT_ready, 1)
            run_experts(dve, expert_dve, 0)
            most_v = dve.value_load(most_i[0:1, 0:1], min_val=0, max_val=SEQ)
            with dve.If(most_v > SLOTS):
                with dve.Fori(1, ROUNDS) as r:
                    dve.wait_ge(pickg_ready, r * (E + 1))
                    nc.vector.tensor_scalar(place[:, :, :], place[:, :, :], -float(SLOTS), None,
                                            ALU.add).then_inc(place_ready, 1)
                    dve.wait_ge(place_ready, r)
                    dve.wait_ge(gh_ready, r * (E + 1))
                    make_pick(0)
                    make_pickg(0)
                    make_bsel(0)
                    take_gather(r * (E + 1))
                    run_experts(dve, expert_dve, r)
                dve.wait_ge(combined, 2 * ROUNDS * E)
            dve.wait_ge(pick_ready, E + 1)
            for t in range(T):
                dve.wait_ge(combined, 2 * E - 1 + t)
                nc.vector.tensor_tensor(resid[:, t, :], resid[:, t, :], bank(2 + 4 * t, 2), ALU.add).then_inc(final_ready, 1)
            dve.wait_ge(fnw_in, 16)
            for t in range(T):
                dve.wait_ge(sumsq_ready, 2 * T + t + 1)
                nc.vector.tensor_scalar(stat[:, 2 + t:3 + t], stat[:, t:t + 1], RMS_EPS, None,
                                        ALU.add).then_inc(var_ready, 1)
                dve.wait_ge(std_ready, 4 + t)
                link(nc.vector.reciprocal(stat[:, 6 + t:7 + t], stat[:, 4 + t:5 + t]))
                nc.vector.scalar_tensor_tensor(resid[:, t, :], resid[:, t, :], stat[:, 6 + t:7 + t], fnw,
                                               ALU.mult, ALU.mult).then_inc(outrow_ready, 1)

        @block.tensor
        def _(pe):
            mm = nc.tensor.matmul
            pe.wait_ge(ident_in, 16)
            for b in range(4):
                t, c0 = b // 2, 4 * (b % 2)
                pe.wait_ge(x_in[t], 16)
                for c in range(4):
                    last = nc.tensor.transpose(bank(b)[:, c * P:(c + 1) * P],
                                               resid[:, t, (c0 + c) * P:(c0 + c + 1) * P], ident)
                last.then_inc(xT_done, 1)

            def project(j):
                pe.wait_ge(slot_full[j], 16)
                if j >= 2:
                    pe.wait_ge(nat_ready, j - 1)
                w = ring[:, j, :].rearrange("p (c n) -> p c n", c=C)
                for t in range(T):
                    if j == 0:
                        pe.wait_ge(hT_ready, 2 * t + 2)
                    for c in range(C):
                        last = mm(bank(4 + j % 2)[:, t * WIN_COLS:(t + 1) * WIN_COLS], hT[:, t, c, :], w[:, c, :],
                                  start=(c == 0), stop=(c == C - 1))
                last.then_inc(chunk_used, 1)

            def transpose_qk(i, j, nr):
                pe.wait_ge(roped, nr)
                if i:
                    pe.wait_ge(qkT_ready, i)
                for a in range(2):
                    for t in range(T):
                        last = nc.tensor.transpose(bank(6)[:, a * SEQ + t * P:a * SEQ + (t + 1) * P],
                                                   nat[:, t, CHUNK_COL[j] + a * P:CHUNK_COL[j] + (a + 1) * P], ident)
                last.then_inc(qkT_done, 1)

            def scores(g):
                for h in (2 * g, 2 * g + 1):
                    r = slice(64 * (h % 2), 64 * (h % 2) + 64)
                    q, k = qkT[r, 4 + h // 2, :], qkT[r, 8 + h // 2, :]
                    if h >= 2:
                        pe.wait_ge(masked, h - 1)
                    mm(bank(h % 2)[:, 0:P], q[:, 0:P], k[:, 0:P], start=True, stop=True)
                    mm(bank(h % 2)[:, P:3 * P], q[:, P:SEQ], k, start=True, stop=True).then_inc(score_done, 1)

            def transpose_prob(g):
                for h in (2 * g, 2 * g + 1):
                    pe.wait_ge(prob_ready, h + 1)
                    for b in range(3):
                        last = nc.tensor.transpose(bank(2 if h % 2 == 0 else 7)[:, b * P:(b + 1) * P],
                                                   prob[:, h % 2, b * P:(b + 1) * P], ident)
                    last.then_inc(probT_done, 1)

            def prob_v(g):
                pe.wait_ge(nat_ready, 6)
                if g:
                    pe.wait_ge(pv_taken, g)
                for h in (2 * g, 2 * g + 1):
                    pe.wait_ge(probT_ready, h + 1)
                    o = bank(3)[64 * (h % 2):64 * (h % 2) + 64, :]
                    v = nat[:, :, MV + h * MOBA_DH:MV + (h + 1) * MOBA_DH]
                    mm(o[:, 0:P], v[:, 0, :], probT[:, h % 2, 0:P], start=True, stop=True)
                    mm(o[:, P:SEQ], v[:, 0, :], probT[:, h % 2, P:2 * P], start=True, stop=False)
                    last = mm(o[:, P:SEQ], v[:, 1, :], probT[:, h % 2, 2 * P:3 * P], start=False, stop=True)
                last.then_inc(pv_done, 1)

            def ret_scores(h):
                r = slice(64 * (h % 2), 64 * (h % 2) + 64)
                q, k = qkT[r, h // 2, :], qkT[r, 2 + h // 2, :]
                if h >= 2:
                    pe.wait_ge(decayed_ready, h - 1)
                mm(bank(6 + h % 2)[:, 0:SEQ], k[:, 0:P], q, start=True, stop=True)
                mm(bank(6 + h % 2)[:, SEQ:SEQ + P], k[:, P:SEQ], q[:, P:SEQ], start=True,
                   stop=True).then_inc(rscore_done, 1)

            def ret_v(h):
                pe.wait_ge(decayed_ready, h + 1)
                cols = slice(h * RET_DV, (h + 1) * RET_DV)
                v = nat[:, :, RV + h * RET_DV:RV + (h + 1) * RET_DV]
                mm(bank(0)[:, cols], decayed[:, h % 2, 0:P], v[:, 0, :], start=True, stop=True)
                mm(bank(1)[:, cols], decayed[:, h % 2, P:2 * P], v[:, 0, :], start=True, stop=False)
                mm(bank(1)[:, cols], decayed[:, h % 2, 2 * P:3 * P], v[:, 1, :], start=False,
                   stop=True).then_inc(ret_done, 1)

            project(0)
            project(1)
            transpose_qk(0, 0, 1)
            project(2)
            transpose_qk(1, 1, 2)
            project(3)
            transpose_qk(2, 2, 3)
            project(4)
            transpose_qk(3, 3, 4)
            project(5)
            pe.wait_ge(qkT_ready, 4)
            scores(0)
            project(6)
            transpose_prob(0)
            scores(1)
            project(7)
            transpose_qk(4, 6, 5)
            prob_v(0)
            transpose_prob(1)
            scores(2)
            project(8)
            transpose_qk(5, 7, 6)
            prob_v(1)
            transpose_prob(2)
            scores(3)
            project(9)
            prob_v(2)
            transpose_prob(3)
            project(10)
            prob_v(3)
            pe.wait_ge(qkT_ready, 6)
            ret_scores(0)
            pe.wait_ge(probT_ready, MOBA_HEADS)
            ret_scores(1)
            project(11)
            pe.wait_ge(masked, MOBA_HEADS)
            ret_v(0)
            ret_v(1)
            ret_scores(2)
            ret_scores(3)

            def wout(s, c, t):
                w = ring[:, WIN_CHUNKS + s, :].rearrange("p (c n) -> p c n", c=2)
                for j in range(2):
                    last = mm(bank(2 + 4 * t + j), mixT[:, c, t * P:(t + 1) * P], w[:, c % 2, j * BANK:(j + 1) * BANK],
                              start=(c == 4), stop=(c == 3))
                return last

            pe.wait_ge(pv_taken, 4)
            ret_v(2)
            ret_v(3)
            for s, pair in enumerate(WOUT_ORDER[0:2]):
                pe.wait_ge(slot_full[WIN_CHUNKS + s], 16)
                for c in (2 * pair, 2 * pair + 1):
                    for t in range(T):
                        last = wout(s, c, t)
                last.then_inc(chunk_used, 1)
            pe.wait_ge(nat_ready, WIN_CHUNKS)
            pe.wait_ge(ret_ready, T)
            for i in range(2):
                for a in range(2):
                    for t in range(T):
                        cols = (2 * i + a) * P
                        last = nc.tensor.transpose(bank(4 + i)[:, a * SEQ + t * P:a * SEQ + (t + 1) * P],
                                                   ret[:, t, cols:cols + P], ident)
                last.then_inc(retT_done, 1)
            pe.wait_ge(retT_ready, 2)
            for s in (2, 3):
                pe.wait_ge(slot_full[WIN_CHUNKS + s], 16)
            for t in range(T):
                for s in (2, 3):
                    for c in (2 * WOUT_ORDER[s], 2 * WOUT_ORDER[s] + 1):
                        last = wout(s, c, t)
                    if t == T - 1:
                        last.then_inc(chunk_used, 1)
                if t == 0:
                    last.then_inc(wout_done, 1)

            for t in range(T):
                pe.wait_ge(x2_ready, t + 1)
                for b in (2 * t, 2 * t + 1):
                    for c in range(4):
                        last = nc.tensor.transpose(bank((0, 1, 4, 5)[b])[:, c * P:(c + 1) * P],
                                                   resid[:, t, (4 * (b % 2) + c) * P:(4 * (b % 2) + c + 1) * P], ident)
                    last.then_inc(h2T_done, 1)
                pe.wait_ge(h2T_ready, 2 * t + 2)
                for c in range(C):
                    last = mm(bank(3 + 4 * t)[:, 0:E], h2T[:, t, c, :], wr[:, c, :], start=(c == 0), stop=(c == C - 1))
                last.then_inc(logits_done, 1)
            before_w, ones_w = count_w[:, 0:P], count_w[:, P:2 * P]
            pe.wait_ge(member_ready, T)
            mm(bank(2)[:, 0:E], before_w, member[:, 0, :], start=True, stop=True)
            mm(bank(2)[:, E:2 * E], ones_w, member[:, 0, :], start=True, stop=False)
            mm(bank(2)[:, E:2 * E], before_w, member[:, 1, :], start=False, stop=True)
            mm(bank(2)[:, 2 * E:3 * E], ones_w, member[:, 0, :], start=True, stop=False)
            mm(bank(2)[:, 2 * E:3 * E], ones_w, member[:, 1, :], start=False, stop=True).then_inc(prefix_done, 1)

            def put_transposes():
                for t in range(T):
                    last = nc.tensor.transpose(bank(4)[:, t * P:(t + 1) * P], pickg[:, t, :], ident)
                last.then_inc(put_done, 1)

            def gather(m):
                pe.wait_ge(pick_ready, m + 1)
                for c in range(C):
                    for t in range(T):
                        last = mm(bank(4)[:, c * SLOTS:(c + 1) * SLOTS], resid[:, t, c * P:(c + 1) * P], pick[:, t, :],
                                  start=(t == 0), stop=(t == T - 1))
                last.then_inc(gather_done, 1)

            def expert_pe(r, i, j):
                e = local_expert(i, j)
                n, m = r * E + e, r * (E + 1) + e
                pe.wait_ge(pickg_ready, m + 1)
                pe.wait_ge(gh_ready, m + 1)
                put_transposes()
                for v in range(2):
                    for half in range(2):
                        mm(bank(v)[64 * half:64 * half + 64, :], bsel[v * E:(v + 1) * E, :],
                           b1_sb[v * E:(v + 1) * E, half * BANK:(half + 1) * BANK], start=True, stop=False)
                for k in range(W1_CHUNKS):
                    s = slot_of(j, k)
                    pe.wait_ge(slot_full[s], slot_count(r, i, j, k))
                    for v in range(2):
                        for half in range(2):
                            last = mm(bank(v)[64 * half:64 * half + 64, :], gh[:, k, :],
                                      ring[:, s, v * F + half * BANK:v * F + (half + 1) * BANK],
                                      start=False, stop=(k == W1_CHUNKS - 1))
                    last.then_inc(chunk_used, 1)
                pe.wait_ge(put_ready, n + 1)
                gather(m + 1)
                if isinstance(r, int) and j == 0:
                    start_accumulators()
                pe.wait_ge(act_ready, n + 1)
                for c in range(4):
                    last = nc.tensor.transpose(bank(5)[:, c * P:(c + 1) * P], a_sb[:, c * P:(c + 1) * P], ident)
                last.then_inc(actT_done, 1)
                pe.wait_ge(actT_ready, n + 1)
                for k in range(W2_CHUNKS):
                    s = slot_of(j, W1_CHUNKS + k)
                    pe.wait_ge(slot_full[s], slot_count(r, i, j, W1_CHUNKS + k))
                    for c in (2 * k, 2 * k + 1):
                        for half in range(2):
                            last = mm(bank(5)[64 * half:64 * half + 64, :],
                                      aT[:, c % 4, 64 * (c // 4):64 * (c // 4) + 64],
                                      ring[:, s, (c % 2) * D + half * BANK:(c % 2) * D + (half + 1) * BANK],
                                      start=(c == 0), stop=(c == C - 1))
                    last.then_inc(chunk_used, 1)
                pe.wait_ge(y_ready, n + 1)
                for t in range(T):
                    for half in range(2):
                        rows = slice(64 * half, 64 * half + 64)
                        last = mm(bank(2 + 4 * t + half), putb[rows, t * P:(t + 1) * P], y_sb[rows, :],
                                  start=False, stop=False, skip_group_check=True)
                    last.then_inc(combined, 1)

            def start_accumulators():
                pe.wait_ge(gatesT_ready, 1)
                for t in range(T):
                    for half in range(2):
                        mm(bank(2 + 4 * t + half), gatesT[:, t * P:(t + 1) * P], b2_sb[:, half * BANK:(half + 1) * BANK],
                           start=True, stop=False, skip_group_check=True)

            pe.wait_ge(h2T_ready, 4)
            gather(0)
            pe.wait_ge(pickg_ready, 1)
            for t in range(T):
                last = nc.tensor.transpose(bank(5)[0:E, t * P:(t + 1) * P], gates[:, t, 0:E], ident)
            last.then_inc(gatesT_done, 1)
            pe.wait_ge(late_in, 48)
            pe.wait_ge(most_ready, 1)
            run_experts(pe, expert_pe, 0)
            most_v = pe.value_load(most_i[0:1, 0:1], min_val=0, max_val=SEQ)
            with pe.If(most_v > SLOTS):
                with pe.Fori(1, ROUNDS) as r:
                    pe.wait_ge(gh_ready, r * (E + 1))
                    gather(r * (E + 1))
                    run_experts(pe, expert_pe, r)


def constants():
    import numpy as np
    f = np.float32
    p = np.arange(P)
    part = {}
    part["ident"] = np.eye(P)
    part["before"] = p[:, None] < p[None, :]
    part["ones"] = np.ones((P, P))
    part["causal"] = np.where(p[None, :] <= p[:, None], 0.0, -1e30)
    log_g = np.log1p(-np.exp2(f(-5.0) - np.arange(RET_HEADS, dtype=f)))
    rel = (np.arange(SEQ)[None, :] - p[:, None]).astype(f)
    dec = np.where(rel >= 0, np.exp(log_g[:, None, None] * np.maximum(rel, 0)), 0) * f(RET_DK ** -0.5)
    part["decay"] = dec.transpose(1, 0, 2).reshape(P, -1)
    part["slot"] = np.tile(np.arange(SLOTS), (P, 2))
    part["row"] = p[:, None] % E == np.arange(E + 1)[None, :]
    for name, dim, theta in (("ret", RET_DK, 10000.0), ("moba", MOBA_ROPE, 500000.0)):
        half = dim // 2
        inv = f(theta) ** (f(-2.0) * np.arange(half, dtype=f) / f(dim))
        ang = np.arange(SEQ, dtype=f)[:, None] * inv[None, :].astype(f)
        cos, sin = np.cos(ang), np.sin(ang)
        for which, tab in (("cos", np.concatenate([cos, cos], 1)), ("sin", np.concatenate([-sin, sin], 1))):
            part[f"{name}_{which}"] = tab.reshape(T, P, dim).transpose(1, 0, 2).reshape(P, -1)
    return np.concatenate([part[n].astype(f) for n, _ in CONST_PARTS], axis=1)


_INS = ["x", "norm1_w", "w_in", "ret_norm_w", "w_out", "norm2_w", "w_router", "b_router",
        "w1", "b1", "w2", "b2", "final_norm_w"]


def kernel(**inputs):
    import numpy as np
    import concourse.bacc as bacc
    from concourse.bass_utils import run_bass_kernel_spmd

    nc = bacc.Bacc("TRN2", target_bir_lowering=False, num_devices=1)
    arrays, args = {}, []
    for name, a in [(n, inputs[n]) for n in _INS] + [("consts", constants())]:
        a = np.ascontiguousarray(a)
        arrays[f"in_{name}"] = a
        args.append(nc.dram_tensor(f"in_{name}", a.shape, mybir.dt.from_np(a.dtype), kind="ExternalInput").ap())
    args.append(nc.dram_tensor("out_0", (1, SEQ, D), F32, kind="ExternalOutput").ap())
    layer_kernel(nc, *args)
    r = run_bass_kernel_spmd(nc, [arrays], core_ids=[0])
    return r.results[0]["out_0"]
```

```python
import concourse.bass as bass
from concourse import mybir
from contextlib import ExitStack

F32 = mybir.dt.float32
BF16 = mybir.dt.bfloat16
I32 = mybir.dt.int32
ALU = mybir.AluOpType
ACT = mybir.ActivationFunctionType
AX = mybir.AxisListType

P = 128
SEQ = 256
T = SEQ // P
D = 1024
C = D // P
RET_HEADS, RET_DK, RET_DV = 4, 64, 128
MOBA_HEADS, MOBA_DH, MOBA_ROPE = 8, 64, 16
D_IN = 3072
E = 32
TOPK = 4
F = 1024
SLOTS = 64
ROUNDS = SEQ // SLOTS
BANK = 512
LIMIT, ALPHA = 7.0, 1.702
RMS_EPS, GN_EPS = 1e-5, 1e-6

RING = 21
SLOT_COLS = 2048
WIN_COLS = SLOT_COLS // C
WIN_CHUNKS = D_IN // WIN_COLS
WOUT_CHUNKS = C // 2
HEAD_CHUNKS = WIN_CHUNKS + WOUT_CHUNKS
W1_CHUNKS = C
W2_CHUNKS = C // 2
EXPERT_CHUNKS = W1_CHUNKS + W2_CHUNKS
ROUND_CHUNKS = E * EXPERT_CHUNKS
PEEL = 3
UNROLL = 7
ITERS = (E - PEEL - 1) // UNROLL
TURNS = UNROLL * EXPERT_CHUNKS // RING
LAST = E - 1
assert PEEL + ITERS * UNROLL + 1 == E and TURNS * RING == UNROLL * EXPERT_CHUNKS
SENTINEL = 3.0e38
LT_BANK, LOGIT_BANK = (3, 0), (1, 4)
WARM_TOPK, WARM_PLACE = 12, 8
WARM_X, WARM_WIN = 16, 24

RQ, RK, RV, RG, MQ, MK, MV = 0, 256, 512, 1024, 1536, 2048, 2560
CHUNK_COL = [MQ, MK, MQ + 256, MK + 256, MV, MV + 256, RQ, RK, RV, RV + 256, RG, RG + 256]
FIRST_ORDER = list(range(12)) + [20, 12, 13, 16, 17, 18, 14, 15, 19]
WOUT_ORDER = [2, 3, 0, 1]

CONST_PARTS = [("ident", P), ("before", P), ("ones", P), ("causal", P), ("decay", RET_HEADS * SEQ),
               ("slot", 2 * SLOTS), ("row", E), ("ret_cos", T * RET_DK), ("ret_sin", T * RET_DK),
               ("moba_cos", T * MOBA_ROPE), ("moba_sin", T * MOBA_ROPE)]
CONST_COLS = sum(n for _, n in CONST_PARTS)


def col(e):
    return slice(e, e + 1) if isinstance(e, int) else bass.ds(e, 1)


def half_cols(half):
    return slice(half * BANK, (half + 1) * BANK)


def local_expert(i, j):
    return i * UNROLL + j


def slot_of(j, k):
    return (j * EXPERT_CHUNKS + k) % RING


def slot_count(r, i, j, k):
    s, g = slot_of(j, k), j * EXPERT_CHUNKS + k
    head = 1 if s < HEAD_CHUNKS else 0
    per_round = len(range(s, ROUND_CHUNKS, RING))
    return 16 * (r * per_round + i * TURNS + (head + g // RING + 1))


def layer_kernel(nc, x, norm1_w, w_in, ret_norm_w, w_out, norm2_w, w_router, b_router,
                 w1, b1, w2, b2, final_norm_w, consts, out):
    x_v = x.rearrange("b (t p) d -> p (b t) d", p=P)
    out_v = out.rearrange("b (t p) d -> p (b t) d", p=P)
    win_v = w_in.rearrange("l (c p) n -> p (l c) n", p=P)
    wout_v = w_out.rearrange("l (c p) n -> p (l c) n", p=P)
    w1_v = w1.rearrange("l e (c p) n -> (l e) c p n", p=P)
    w2_v = w2.rearrange("l e (c p) n -> (l e) p c n", p=P)

    ctx = ExitStack()
    with ctx:
        def sb(name, shape, dt=F32):
            return ctx.enter_context(nc.sbuf_tensor(name, shape, dt))

        def sem(name):
            return ctx.enter_context(nc.semaphore(name))

        ctx.enter_context(nc.allow_non_contiguous_dma(reason="norm weights, one element per partition and tile"))
        PS = ctx.enter_context(nc.psum_tensor("PS", [P, 8 * BANK], F32))

        def bank(b, n=1):
            return PS[:, b * BANK:(b + n) * BANK]

        ring = sb("ring", [P, RING, SLOT_COLS])
        cst = sb("cst", [P, CONST_COLS])
        resid = sb("resid", [P, T, D])
        work = sb("work", [P, 12 * SEQ + 4 * 3 * P])
        nat_flat = ring[:, HEAD_CHUNKS:HEAD_CHUNKS + 3, :].rearrange("p s n -> p (s n)")
        nat = nat_flat.rearrange("p (t n) -> p t n", t=T)
        mixT = ring[:, HEAD_CHUNKS + 3, :].rearrange("p (c n) -> p c n", c=C)
        hT = ring[:, HEAD_CHUNKS + 4, :].rearrange("p (t c n) -> p t c n", t=T, c=C)
        n1w = sb("n1w", [P, C])
        n2w = sb("n2w", [P, C])
        brb = sb("brb", [P, E])
        wr = sb("wr", [P, C, E])
        stat = sb("stat", [P, 64])
        bn = sb("bn", [P, T * RET_HEADS, 6])
        gn = sb("gn", [P, T * RET_HEADS, 2])
        gn_rstd = sb("gn_rstd", [P, T * RET_HEADS])
        logits = sb("logits", [P, T, E + TOPK])
        marked = sb("marked", [P, T, E + TOPK])
        expl = sb("expl", [P, T, E])
        top = sb("top", [P, T, 8])
        gates = sb("gates", [P, T, E])
        member = sb("member", [P, T, E], BF16)
        count_w = sb("count_w", [P, 2 * P], BF16)
        warm_w = sb("warm_w", [P, 2 * P], BF16)
        place = sb("place", [P, T, E])
        most = sb("most", [P, 1])
        most_i = sb("most_i", [1, 1], I32)

        c_at, at = {}, 0
        for name, n in CONST_PARTS:
            c_at[name] = cst[:, at:at + n]
            at += n
        ident, before, ones, causal = (c_at[n] for n in ("ident", "before", "ones", "causal"))
        decay = c_at["decay"].rearrange("p (h n) -> p h n", h=RET_HEADS)
        slot_id = c_at["slot"]
        row_id = c_at["row"]
        ret_cos = c_at["ret_cos"].rearrange("p (t d) -> p t d", t=T)
        ret_sin = c_at["ret_sin"].rearrange("p (t d) -> p t d", t=T)
        moba_cos = c_at["moba_cos"].rearrange("p (t d) -> p t d", t=T)
        moba_sin = c_at["moba_sin"].rearrange("p (t d) -> p t d", t=T)

        qkT = work[:, 0:12 * SEQ].rearrange("p (i n) -> p i n", n=SEQ)
        prob = work[:, 3072:3840].rearrange("p (s n) -> p s n", s=2)
        probT = work[:, 3840:4608].rearrange("p (s n) -> p s n", s=2)
        decayed = prob
        retw = nat[:, 0, MQ:MQ + 512]
        ret = nat[:, :, RQ:RQ + 512]

        h2T = work[:, 0:2048].rearrange("p (t c n) -> p t c n", t=T, c=C)
        lT = work[:, 3072:3328].rearrange("p (t n) -> p t n", t=T)
        b1_sb = work[0:2 * E, 3328:4352]
        b2_sb = work[2 * E:3 * E, 3328:4352]
        dump = work[:, 2048:2048 + D]
        dump_end = work[:, 1280:1280 + D]
        fnw_slot = ROUND_CHUNKS % RING
        fnw = ring[:, fnw_slot, 0:D]
        gh = work[:, 0:512].rearrange("p (c s) -> p c s", c=C)
        pick = work[:, 512:640].rearrange("p (t s) -> p t s", t=T)
        pickg = work[:, 640:896].rearrange("p (t s) -> p t s", t=T)
        putb = work[:, 896:1152]
        bsel = work[0:2 * E, 1152:1216]
        g_sb = work[:, 1280:1792]
        a_sb = work[:, 1792:2304]
        s_sb = work[:, 2304:2816]
        aT = work[:, 2816:3328].rearrange("p (c n) -> p c n", c=4)
        y_sb = work[:, 2816:3328]

        scr = sb("scr", [P, 256])
        gsig = nat[:, :, MK:MK + 512]
        gatesT = scr[2 * E:3 * E, 0:SEQ]

        slot_full = [sem(f"slot_full{s}") for s in range(RING)]
        chunk_used = sem("chunk_used")
        x_in = [sem(f"x_in{t}") for t in range(T)]
        cst_in = sem("cst_in")
        ident_in = sem("ident_in")
        n1w_in = sem("n1w_in")
        small_in = sem("small_in")
        fnw_in = sem("fnw_in")
        warm_w_ready = sem("warm_w_ready")
        one_ready = sem("one_ready")
        retw_in = sem("retw_in")
        late_in = sem("late_in")
        out_done = sem("out_done")
        sumsq_ready = sem("sumsq_ready")
        var_ready = sem("var_ready")
        std_ready = sem("std_ready")
        rstd_ready = sem("rstd_ready")
        xT_done = sem("xT_done")
        hT_ready = sem("hT_ready")
        nat_ready = sem("nat_ready")
        roped = sem("roped")
        qkT_done = sem("qkT_done")
        qkT_ready = sem("qkT_ready")
        score_done = sem("score_done")
        masked = sem("masked")
        negmax_ready = sem("negmax_ready")
        exp_ready = sem("exp_ready")
        prob_ready = sem("prob_ready")
        probT_done = sem("probT_done")
        probT_ready = sem("probT_ready")
        pv_done = sem("pv_done")
        pv_taken = sem("pv_taken")
        rscore_done = sem("rscore_done")
        decayed_ready = sem("decayed_ready")
        ret_done = sem("ret_done")
        siglu_ready = sem("siglu_ready")
        gnvar_ready = sem("gnvar_ready")
        gnstd_ready = sem("gnstd_ready")
        ret_ready = sem("ret_ready")
        retT_done = sem("retT_done")
        retT_ready = sem("retT_ready")
        wout_done = sem("wout_done")
        x2_ready = sem("x2_ready")
        h2T_done = sem("h2T_done")
        wr_ready = sem("wr_ready")
        h2T0_ready = sem("h2T0_ready")
        h2T1_ready = sem("h2T1_ready")
        lT_done = sem("lT_done")
        lT_ready = sem("lT_ready")
        logits_done = sem("logits_done")
        top_ready = sem("top_ready")
        topexp_ready = sem("topexp_ready")
        member_ready = sem("member_ready")
        prefix_done = sem("prefix_done")
        gatesT_done = sem("gatesT_done")
        gatesT_ready = sem("gatesT_ready")
        place_ready = sem("place_ready")
        most_ready = sem("most_ready")
        dve_step = sem("dve_step")
        pick_ready = sem("pick_ready")
        pickg_ready = sem("pickg_ready")
        put_done = sem("put_done")
        put_ready = sem("put_ready")
        gather0_done = sem("gather0_done")
        gather_done = sem("gather_done")
        gh0_ready = sem("gh0_ready")
        gh_ready = sem("gh_ready")
        gate_ready = sem("gate_ready")
        lin_ready = sem("lin_ready")
        glin_ready = sem("glin_ready")
        sig_ready = sem("sig_ready")
        act_ready = sem("act_ready")
        actT_done = sem("actT_done")
        actT_ready = sem("actT_ready")
        y_ready = sem("y_ready")
        combined = sem("combined")
        final_ready = sem("final_ready")
        out_ready = sem("out_ready")

        def run_experts(eng, expert, r):
            for j in range(PEEL):
                expert(r, 0, j)
            with eng.Fori(0, ITERS) as i:
                for j in range(PEEL, PEEL + UNROLL):
                    expert(r, i, j)
            expert(r, 0, LAST)

        def up_done(n):
            return n * EXPERT_CHUNKS + (HEAD_CHUNKS + W1_CHUNKS)

        def down_done(n):
            return n * EXPERT_CHUNKS + (HEAD_CHUNKS + EXPERT_CHUNKS)

        block = ctx.enter_context(nc.Block())

        @block.sync
        def _(sp):
            for t in range(T):
                sp.dma_start(resid[:, t, :], x_v[:, t, :]).then_inc(x_in[t], 16)
            for j, col in enumerate(CHUNK_COL):
                dst = ring[:, j, :].rearrange("p (c n) -> p c n", c=C)
                sp.dma_start(dst, win_v[:, :, col:col + WIN_COLS]).then_inc(slot_full[j], 16)
            for j, pair in enumerate(WOUT_ORDER):
                s = WIN_CHUNKS + j
                dst = ring[:, s, :].rearrange("p (c n) -> p c n", c=2)
                sp.dma_start(dst, wout_v[:, 2 * pair:2 * pair + 2, :]).then_inc(slot_full[s], 16)

            def load(r, i, j, k):
                e, s = local_expert(i, j), slot_of(j, k)
                if k < W1_CHUNKS:
                    sp.dma_start(ring[:, s, :], w1_v[e, k, :, :]).then_inc(slot_full[s], 16)
                else:
                    c = 2 * (k - W1_CHUNKS)
                    dst = ring[:, s, :].rearrange("p (c n) -> p c n", c=2)
                    sp.dma_start(dst, w2_v[e, :, c:c + 2, :]).then_inc(slot_full[s], 16)

            for g in FIRST_ORDER:
                if g < HEAD_CHUNKS:
                    sp.wait_ge(chunk_used, g + 1)
                elif g == HEAD_CHUNKS + 4:
                    sp.wait_ge(chunk_used, WIN_CHUNKS)
                elif g < HEAD_CHUNKS + 3:
                    sp.wait_ge(retT_done, 2)
                else:
                    sp.wait_ge(chunk_used, HEAD_CHUNKS)
                load(0, 0, g // EXPERT_CHUNKS, g % EXPERT_CHUNKS)

            def expert_loads(r, i, j):
                for k in range(EXPERT_CHUNKS):
                    g = j * EXPERT_CHUNKS + k
                    if g < RING:
                        if isinstance(r, int):
                            continue
                        sp.wait_ge(chunk_used, r * ROUND_CHUNKS + HEAD_CHUNKS)
                    else:
                        sp.wait_ge(chunk_used, r * ROUND_CHUNKS + i * (UNROLL * EXPERT_CHUNKS)
                                   + (HEAD_CHUNKS + g - RING + 1))
                    load(r, i, j, k)

            run_experts(sp, expert_loads, 0)
            sp.wait_ge(most_ready, 1)
            most_v = sp.value_load(most_i[0:1, 0:1], min_val=0, max_val=SEQ)
            with sp.If(most_v > SLOTS):
                with sp.Fori(1, ROUNDS) as r:
                    run_experts(sp, expert_loads, r)
                sp.wait_ge(chunk_used, ROUNDS * ROUND_CHUNKS + HEAD_CHUNKS)
            sp.wait_ge(chunk_used, ROUND_CHUNKS + HEAD_CHUNKS - RING + 1)
            sp.dma_start(fnw, final_norm_w.rearrange("(a n) -> a n", a=1).broadcast_to([P, D])).then_inc(fnw_in, 16)
            for k in range(2 * T):
                t, cols = k // 2, half_cols(k % 2)
                sp.wait_ge(out_ready, k + 1)
                sp.dma_start(out_v[:, t, cols], resid[:, t, cols]).then_inc(out_done, 16)
            sp.wait_ge(out_done, 16 * 2 * T)

        @block.gpsimd
        def _(pool):
            pool.wait_ge(qkT_done, 4)
            pool.dma_start(retw, ret_norm_w.broadcast_to([P, 512])).then_inc(retw_in, 16)
            pool.wait_ge(probT_ready, MOBA_HEADS)
            pool.wait_ge(pv_done, 4)
            pool.wait_ge(ret_done, RET_HEADS)
            for v in range(2):
                pool.dma_start(b1_sb[v * E:(v + 1) * E, :], b1[0, :, v * F:(v + 1) * F]).then_inc(late_in, 16)
            pool.dma_start(b2_sb, b2[0, :, :]).then_inc(late_in, 16)
            pool.wait_ge(late_in, 48)

        @block.scalar
        def _(act):
            act.dma_start(ident, consts[:, 0:P]).then_inc(ident_in, 16)
            act.dma_start(n1w[:, :], norm1_w.rearrange("l (c p) -> p (l c)", p=P)).then_inc(n1w_in, 16)
            act.dma_start(cst[:, P:], consts[:, P:]).then_inc(cst_in, 16)
            act.dma_start(n2w[:, :], norm2_w.rearrange("l (c p) -> p (l c)", p=P)).then_inc(small_in, 16)
            act.dma_start(brb[:, :], b_router.broadcast_to([P, E])).then_inc(small_in, 16)
            act.dma_start(wr[:, :, :], w_router.rearrange("l (c p) n -> p (l c) n", p=P)).then_inc(small_in, 16)

            act.wait_ge(one_ready, 1)
            nc.scalar.activation(stat[:, 63:64], stat[:, 62:63], ACT.Sqrt)
            for t in range(T):
                act.wait_ge(x_in[t], 16)
                if t:
                    act.wait_ge(sumsq_ready, t)
                nc.scalar.activation(work[:, 0:D], resid[:, t, :], ACT.Square, scale=1.0 / 32.0,
                                     accum_out=stat[:, t:t + 1]).then_inc(sumsq_ready, 1)
            act.wait_ge(var_ready, 1)
            nc.scalar.activation(stat[:, 4:6], stat[:, 2:4], ACT.Sqrt).then_inc(std_ready, 1)

            def take_proj(j):
                act.wait_ge(chunk_used, j + 1)
                c0 = CHUNK_COL[j]
                for t in range(T):
                    ins = nc.scalar.activation(nat[:, t, c0:c0 + WIN_COLS],
                                               bank(4 + j % 2)[:, t * WIN_COLS:(t + 1) * WIN_COLS], ACT.Copy,
                                               scale=stat[:, 6 + t:7 + t])
                ins.then_inc(nat_ready, 1)

            def exps(g):
                for h in (2 * g, 2 * g + 1):
                    act.wait_ge(negmax_ready, h + 1)
                    for t, (a, b) in enumerate(((0, P), (P, 3 * P))):
                        nc.scalar.activation(prob[:, h % 2, a:b], prob[:, h % 2, a:b], ACT.Exp,
                                             bias=stat[:, 8 + 2 * (h % 2) + t:9 + 2 * (h % 2) + t],
                                             scale=MOBA_DH ** -0.5,
                                             accum_out=stat[:, 12 + 2 * (h % 2) + t:13 + 2 * (h % 2) + t]
                                             ).then_inc(exp_ready, 1)

            act.wait_ge(rstd_ready, 1)
            for j in range(6):
                take_proj(j)
            exps(0)
            take_proj(6)
            exps(1)
            take_proj(7)
            exps(2)
            take_proj(8)
            exps(3)
            take_proj(9)
            take_proj(10)
            take_proj(11)
            act.wait_ge(nat_ready, WIN_CHUNKS)
            for t in range(T):
                nc.scalar.activation(gsig[:, t, :], nat[:, t, RG:RG + 512], ACT.Sigmoid).then_inc(siglu_ready, 1)
            act.wait_ge(gnvar_ready, 1)
            nc.scalar.activation(gn_rstd[:, :], gn_rstd[:, :], ACT.Sqrt).then_inc(gnstd_ready, 1)
            for t in range(T):
                if t == 1:
                    for b in range(2):
                        act.wait_ge(h2T_done, b + 1)
                        nc.scalar.activation(h2T[:, 0, 4 * b:4 * b + 4, :], bank(b).rearrange("p (c n) -> p c n", c=4),
                                             ACT.Copy).then_inc(h2T0_ready, 1)
                act.wait_ge(x2_ready, t + 1)
                act.wait_ge(sumsq_ready, T + t)
                nc.scalar.activation(dump, resid[:, t, :], ACT.Square, scale=1.0 / 32.0,
                                     accum_out=stat[:, t:t + 1]).then_inc(sumsq_ready, 1)
                act.wait_ge(var_ready, 2 + t)
                nc.scalar.activation(stat[:, 4 + t:5 + t], stat[:, 2 + t:3 + t], ACT.Sqrt).then_inc(std_ready, 1)
            for t in range(T):
                act.wait_ge(top_ready, 1)
                nc.scalar.activation(expl[:, t, :], logits[:, t, 0:E], ACT.Exp,
                                     bias=stat[:, 20 + t:21 + t]).then_inc(topexp_ready, 1)

            def expert_act(r, i, j):
                n = r * E + local_expert(i, j)
                act.wait_ge(gate_ready, n + 1)
                nc.scalar.activation(s_sb, g_sb, ACT.Sigmoid, scale=ALPHA).then_inc(sig_ready, 1)
                act.wait_ge(actT_done, n + 1)
                nc.scalar.activation(aT, bank(5).rearrange("p (c n) -> p c n", c=4), ACT.Copy).then_inc(actT_ready, 1)
                act.wait_ge(chunk_used, down_done(n))
                nc.scalar.activation(y_sb, bank(5), ACT.Copy).then_inc(y_ready, 1)

            run_experts(act, expert_act, 0)
            act.wait_ge(most_ready, 1)
            most_v = act.value_load(most_i[0:1, 0:1], min_val=0, max_val=SEQ)
            with act.If(most_v > SLOTS):
                with act.Fori(1, ROUNDS) as r:
                    run_experts(act, expert_act, r)
            nc.scalar.activation(stat[:, 61:62], stat[:, 62:63], ACT.Sqrt)
            def final_std(t):
                act.wait_ge(var_ready, 4 + t)
                nc.scalar.activation(stat[:, 4 + t:5 + t], stat[:, 2 + t:3 + t], ACT.Sqrt).then_inc(std_ready, 1)

            for k in range(2 * T):
                act.wait_ge(final_ready, k + 1)
                act.wait_ge(sumsq_ready, 2 * T + k)
                nc.scalar.activation(dump_end[:, 0:BANK], resid[:, k // 2, half_cols(k % 2)], ACT.Square,
                                     scale=1.0 / 32.0, accum_out=stat[:, 32 + k:33 + k]).then_inc(sumsq_ready, 1)
                if k >= 2:
                    final_std(k - 2)

        @block.vector
        def _(dve):
            steps = [0]

            def link(ins):
                steps[0] += 1
                ins.then_inc(dve_step, 1)
                dve.wait_ge(dve_step, steps[0])

            nc.vector.memset(warm_w[:, :], 1.0).then_inc(warm_w_ready, 1)
            nc.vector.memset(stat[:, 62:63], 1.0).then_inc(one_ready, 1)
            link(nc.vector.memset(logits[:, :, :], -SENTINEL))

            def w_cols(w, c0):
                return w[:, c0:c0 + 4].unsqueeze(2).broadcast_to([P, 4, P])

            dve.wait_ge(n1w_in, 16)
            for b in range(4):
                t, c0 = b // 2, 4 * (b % 2)
                dve.wait_ge(xT_done, b + 1)
                nc.vector.tensor_tensor(hT[:, t, c0:c0 + 4, :], bank(b).rearrange("p (c n) -> p c n", c=4),
                                        w_cols(n1w, c0), ALU.mult).then_inc(hT_ready, 1)
            dve.wait_ge(sumsq_ready, T)
            nc.vector.tensor_scalar(stat[:, 2:4], stat[:, 0:2], RMS_EPS, None, ALU.add).then_inc(var_ready, 1)
            dve.wait_ge(std_ready, 1)
            nc.vector.reciprocal(stat[:, 6:8], stat[:, 4:6]).then_inc(rstd_ready, 1)
            dve.wait_ge(cst_in, 16)
            nc.vector.tensor_copy(count_w[:, :], cst[:, P:3 * P])

            rotations = [0]

            def rope(j):
                dve.wait_ge(nat_ready, j + 1)
                if rotations[0]:
                    dve.wait_ge(roped, rotations[0])
                rotations[0] += 1
                retention = CHUNK_COL[j] in (RQ, RK)
                dim = RET_DK if retention else MOBA_ROPE
                cos, sin = (ret_cos, ret_sin) if retention else (moba_cos, moba_sin)
                half, heads = dim // 2, WIN_COLS // 64
                for t in range(T):
                    v = nat[:, t, CHUNK_COL[j]:CHUNK_COL[j] + WIN_COLS].rearrange("p (h d) -> p h d", h=heads)
                    swapped = scr[:, 0:heads * dim].rearrange("p (h d) -> p h d", h=heads)

                    def table(tab, a, b):
                        return tab[:, t, a:b].unsqueeze(1).broadcast_to([P, heads, b - a])

                    nc.vector.tensor_tensor(swapped[:, :, 0:half], v[:, :, half:dim], table(sin, 0, half), ALU.mult)
                    link(nc.vector.tensor_tensor(swapped[:, :, half:dim], v[:, :, 0:half], table(sin, half, dim),
                                                 ALU.mult))
                    link(nc.vector.tensor_tensor(v[:, :, 0:dim], v[:, :, 0:dim], table(cos, 0, dim), ALU.mult))
                    ins = nc.vector.tensor_tensor(v[:, :, 0:dim], v[:, :, 0:dim], swapped, ALU.add)
                    if t == 0:
                        link(ins)
                ins.then_inc(roped, 1)

            def take_qkT(i, tile):
                dve.wait_ge(qkT_done, i + 1)
                nc.vector.tensor_copy(qkT[:, tile:tile + 2, :],
                                      bank(6).rearrange("p (i n) -> p i n", i=2)).then_inc(qkT_ready, 1)

            def mask_max(g):
                for h in (2 * g, 2 * g + 1):
                    s = bank(h % 2)
                    diag = s[:, 0:3 * P].rearrange("p (b n) -> p b n", b=3)[:, 0:3:2, :]
                    pdiag = prob[:, h % 2, :].rearrange("p (b n) -> p b n", b=3)[:, 0:3:2, :]
                    dve.wait_ge(score_done, h + 1)
                    nc.vector.tensor_tensor(pdiag, diag, causal.unsqueeze(1).broadcast_to([P, 2, P]), ALU.add)
                    nc.vector.tensor_copy(prob[:, h % 2, P:2 * P], s[:, P:2 * P]).then_inc(masked, 1)
                    dve.wait_ge(masked, h + 1)
                    if h >= 2:
                        dve.wait_ge(negmax_ready, h - 1)
                    m = stat[:, 16 + 2 * (h % 2):18 + 2 * (h % 2)]
                    nc.vector.reduce_max(m[:, 0:1], prob[:, h % 2, 0:P], AX.X)
                    link(nc.vector.reduce_max(m[:, 1:2], prob[:, h % 2, P:3 * P], AX.X))
                    nc.vector.tensor_scalar(stat[:, 8 + 2 * (h % 2):10 + 2 * (h % 2)], m, -MOBA_DH ** -0.5, None,
                                            ALU.mult).then_inc(negmax_ready, 1)

            def normalise(g):
                for h in (2 * g, 2 * g + 1):
                    dve.wait_ge(exp_ready, 2 * h + 2)
                    if h >= 2:
                        dve.wait_ge(prob_ready, h - 1)
                    r = stat[:, 28 + 2 * (h % 2):30 + 2 * (h % 2)]
                    link(nc.vector.reciprocal(r, stat[:, 12 + 2 * (h % 2):14 + 2 * (h % 2)]))
                    nc.vector.tensor_scalar(prob[:, h % 2, 0:P], prob[:, h % 2, 0:P], r[:, 0:1], None, ALU.mult)
                    nc.vector.tensor_scalar(prob[:, h % 2, P:3 * P], prob[:, h % 2, P:3 * P], r[:, 1:2], None,
                                            ALU.mult).then_inc(prob_ready, 1)

            def take_probT(g):
                for h in (2 * g, 2 * g + 1):
                    dve.wait_ge(probT_done, h + 1)
                    nc.vector.tensor_copy(probT[:, h % 2, :], bank(2 if h % 2 == 0 else 7)[:, 0:3 * P]
                                          ).then_inc(probT_ready, 1)

            def take_pv(g):
                dve.wait_ge(pv_done, g + 1)
                nc.vector.tensor_copy(mixT[:, 4 + g, :], bank(3)[:, 0:SEQ]).then_inc(pv_taken, 1)

            rope(0)
            rope(1)
            take_qkT(0, 4)
            rope(2)
            take_qkT(1, 8)
            rope(3)
            take_qkT(2, 6)
            take_qkT(3, 10)
            mask_max(0)
            normalise(0)
            take_probT(0)
            mask_max(1)
            normalise(1)
            rope(6)
            take_qkT(4, 0)
            take_pv(0)
            take_probT(1)
            mask_max(2)
            normalise(2)
            rope(7)
            take_qkT(5, 2)
            take_pv(1)
            take_probT(2)
            mask_max(3)
            normalise(3)
            take_pv(2)
            take_probT(3)
            take_pv(3)
            for h in range(RET_HEADS):
                dve.wait_ge(rscore_done, h + 1)
                if h >= 2:
                    dve.wait_ge(ret_done, h - 1)
                s = bank(6 + h % 2)
                nc.vector.tensor_tensor(decayed[:, h % 2, 0:SEQ], s[:, 0:SEQ], decay[:, h, :], ALU.mult)
                nc.vector.tensor_tensor(decayed[:, h % 2, SEQ:SEQ + P], s[:, SEQ:SEQ + P], decay[:, h, 0:P],
                                        ALU.mult).then_inc(decayed_ready, 1)
            dve.wait_ge(retw_in, 16)
            dve.wait_ge(nat_ready, WIN_CHUNKS)
            dve.wait_ge(siglu_ready, T)
            for t in range(T):
                link(nc.vector.tensor_tensor(nat[:, t, RG:RG + 512], nat[:, t, RG:RG + 512], gsig[:, t, :], ALU.mult))
                link(nc.vector.tensor_tensor(nat[:, t, RG:RG + 512], nat[:, t, RG:RG + 512], retw, ALU.mult))
            dve.wait_ge(ret_done, RET_HEADS)
            for t in range(T):
                for h in range(RET_HEADS):
                    nc_in = bank(t)[:, h * RET_DV:(h + 1) * RET_DV]
                    ins = nc.vector.bn_stats(bn[:, t * RET_HEADS + h, :], nc_in)
            link(ins)
            for g in range(T * RET_HEADS):
                ins = nc.vector.bn_aggr(gn[:, g, :], bn[:, g, :])
            link(ins)
            nc.vector.tensor_scalar(gn_rstd[:, :], gn[:, :, 1], GN_EPS, None, ALU.add).then_inc(gnvar_ready, 1)
            dve.wait_ge(gnstd_ready, 1)
            link(nc.vector.reciprocal(gn_rstd[:, :], gn_rstd[:, :]))
            for t in range(T):
                for h in range(RET_HEADS):
                    g = t * RET_HEADS + h
                    ins = nc.vector.tensor_scalar(ret[:, t, h * RET_DV:(h + 1) * RET_DV],
                                                  bank(t)[:, h * RET_DV:(h + 1) * RET_DV],
                                                  gn[:, g, 0:1], gn_rstd[:, g:g + 1], ALU.subtract, ALU.mult)
                link(ins)
                nc.vector.tensor_tensor(ret[:, t, :], ret[:, t, :], nat[:, t, RG:RG + 512],
                                        ALU.mult).then_inc(ret_ready, 1)
            for i in range(2):
                dve.wait_ge(retT_done, i + 1)
                nc.vector.tensor_copy(mixT[:, 2 * i:2 * i + 2, :],
                                      bank(4 + i).rearrange("p (i n) -> p i n", i=2)).then_inc(retT_ready, 1)
            dve.wait_ge(small_in, 48)
            nc.vector.tensor_tensor(wr[:, :, :], wr[:, :, :], n2w[:, :].unsqueeze(2).broadcast_to([P, C, E]),
                                    ALU.mult).then_inc(wr_ready, 1)

            def rms_var(t):
                dve.wait_ge(sumsq_ready, T + t + 1)
                nc.vector.tensor_scalar(stat[:, 2 + t:3 + t], stat[:, t:t + 1], RMS_EPS, None,
                                        ALU.add).then_inc(var_ready, 1)

            def rms_reciprocal(t):
                dve.wait_ge(std_ready, 2 + t)
                return nc.vector.reciprocal(stat[:, 6 + t:7 + t], stat[:, 4 + t:5 + t])

            def take_lT(t):
                dve.wait_ge(lT_done, t + 1)
                nc.vector.tensor_copy(lT[:, t, :], bank(LT_BANK[t])[:, 0:P]).then_inc(lT_ready, 1)

            dve.wait_ge(wout_done, 1)
            nc.vector.tensor_tensor(resid[:, 0, :], resid[:, 0, :], bank(2, 2), ALU.add).then_inc(x2_ready, 1)
            rms_var(0)
            rms_reciprocal(0)
            dve.wait_ge(chunk_used, HEAD_CHUNKS)
            nc.vector.tensor_tensor(resid[:, 1, :], resid[:, 1, :], bank(6, 2), ALU.add).then_inc(x2_ready, 1)
            for b in range(2):
                dve.wait_ge(h2T_done, b + 3)
                nc.vector.tensor_copy(h2T[:, 1, 4 * b:4 * b + 4, :],
                                      bank(6 + b).rearrange("p (c n) -> p c n", c=4)).then_inc(h2T1_ready, 1)
            take_lT(0)
            rms_var(1)
            take_lT(1)
            link(rms_reciprocal(1))
            for t in range(T):
                dve.wait_ge(logits_done, t + 1)
                ins = nc.vector.scalar_tensor_tensor(logits[:, t, 0:E], bank(LOGIT_BANK[t])[:, 0:E],
                                                     stat[:, 6 + t:7 + t], brb[:, :], ALU.mult, ALU.add)
            link(ins)
            for t in range(T):
                ins = nc.vector.max(top[:, t, :], logits[:, t, 0:E])
            link(ins)
            nc.vector.tensor_scalar(stat[:, 20:22], top[:, :, 0], -1.0, None, ALU.mult).then_inc(top_ready, 1)
            dve.wait_ge(top_ready, 1)
            link(nc.vector.memset(top[:, :, TOPK:8], -SENTINEL))
            for t in range(T):
                ins = nc.vector.match_replace(marked[:, t, :], top[:, t, :], logits[:, t, :], SENTINEL)
            link(ins)
            nc.vector.tensor_scalar(member[:, :, :], marked[:, :, 0:E], SENTINEL, None,
                                    ALU.is_equal).then_inc(member_ready, 1)
            dve.wait_ge(member_ready, 1)
            dve.wait_ge(prefix_done, 1)
            link(nc.vector.scalar_tensor_tensor(place[:, :, 0:E], bank(2)[:, 0:T * E].rearrange("p (t e) -> p t e", t=T),
                                                1.0, member[:, :, :], ALU.add, ALU.mult))
            link(nc.vector.tensor_scalar(place[:, :, 0:E], place[:, :, 0:E], -1.0, None, ALU.add))

            def make_pick(e):
                for t in range(T):
                    ins = nc.vector.tensor_scalar(pick[:, t, :], slot_id[:, 0:SLOTS], place[:, t, col(e)],
                                                  stat[:, 6 + t:7 + t], ALU.is_equal, ALU.mult)
                ins.then_inc(pick_ready, 1)

            def make_pickg(e):
                for t in range(T):
                    ins = nc.vector.tensor_scalar(pickg[:, t, :], slot_id, place[:, t, col(e)], gates[:, t, col(e)],
                                                  ALU.is_equal, ALU.mult)
                ins.then_inc(pickg_ready, 1)

            def make_bsel(e):
                nc.vector.tensor_copy(bsel, row_id[0:2 * E, col(e)].broadcast_to([2 * E, SLOTS]))

            def take_gather(n):
                dve.wait_ge(gather_done, n)
                nc.vector.tensor_tensor(gh, bank(4).rearrange("p (c s) -> p c s", c=C),
                                        n2w[:, :].unsqueeze(2).broadcast_to([P, C, SLOTS]), ALU.mult
                                        ).then_inc(gh_ready, 1)

            def take_put(n):
                dve.wait_ge(put_done, n)
                nc.vector.tensor_copy(putb, bank(4)[:, 0:SEQ]).then_inc(put_ready, 1)

            def expert_dve(r, i, j):
                e = local_expert(i, j)
                n = r * E + e
                if j > 0:
                    take_put(n)
                make_pickg(e)
                if j < LAST:
                    if j > 0 or not isinstance(r, int):
                        dve.wait_ge(gather_done, n)
                    make_pick(e + 1)
                dve.wait_ge(chunk_used, up_done(n))
                nc.vector.tensor_scalar(g_sb, bank(0), LIMIT, None, ALU.min).then_inc(gate_ready, 1)
                nc.vector.tensor_scalar(a_sb, bank(1), LIMIT, -LIMIT, ALU.min, ALU.max).then_inc(lin_ready, 1)
                dve.wait_ge(gate_ready, n + 1)
                dve.wait_ge(lin_ready, n + 1)
                nc.vector.scalar_tensor_tensor(a_sb, a_sb, 1.0, g_sb, ALU.add, ALU.mult).then_inc(glin_ready, 1)
                dve.wait_ge(glin_ready, n + 1)
                dve.wait_ge(sig_ready, n + 1)
                nc.vector.tensor_tensor(a_sb, a_sb, s_sb, ALU.mult).then_inc(act_ready, 1)
                if j < LAST:
                    make_bsel(e + 1)
                    take_gather(n + 1)
                else:
                    take_put(n + 1)

            def softmax(t):
                dve.wait_ge(topexp_ready, t + 1)
                link(nc.vector.scalar_tensor_tensor(gates[:, t, 0:E], marked[:, t, 0:E], SENTINEL, expl[:, t, :],
                                                    ALU.is_equal, ALU.mult))
                link(nc.vector.reduce_sum(stat[:, 24 + t:25 + t], gates[:, t, 0:E], AX.X))
                link(nc.vector.reciprocal(stat[:, 26 + t:27 + t], stat[:, 24 + t:25 + t]))
                link(nc.vector.tensor_scalar(gates[:, t, 0:E], gates[:, t, 0:E], stat[:, 26 + t:27 + t], None, ALU.mult))

            def take_gather0(half):
                dve.wait_ge(gather0_done, half + 1)
                return nc.vector.tensor_tensor(gh[:, 4 * half:4 * half + 4, :],
                                               bank(4 + half)[:, 0:4 * SLOTS].rearrange("p (c s) -> p c s", c=4),
                                               n2w[:, 4 * half:4 * half + 4].unsqueeze(2).broadcast_to([P, 4, SLOTS]),
                                               ALU.mult)

            make_pick(0)
            make_bsel(0)
            softmax(0)
            take_gather0(0).then_inc(gh0_ready, 1)
            softmax(1)
            take_gather0(1).then_inc(gh_ready, 1)
            link(nc.vector.reduce_max(most[:, :], bank(2)[:, T * E:(T + 1) * E], AX.X))
            nc.vector.tensor_copy(most_i[:, :], most[0:1, :]).then_inc(most_ready, 1)
            dve.wait_ge(gatesT_done, 1)
            nc.vector.tensor_copy(gatesT, bank(7)[0:E, 0:SEQ]).then_inc(gatesT_ready, 1)
            run_experts(dve, expert_dve, 0)
            most_v = dve.value_load(most_i[0:1, 0:1], min_val=0, max_val=SEQ)
            with dve.If(most_v > SLOTS):
                with dve.Fori(1, ROUNDS) as r:
                    dve.wait_ge(pick_ready, r * E)
                    dve.wait_ge(pickg_ready, r * E)
                    nc.vector.tensor_scalar(place[:, :, :], place[:, :, :], -float(SLOTS), None,
                                            ALU.add).then_inc(place_ready, 1)
                    dve.wait_ge(place_ready, r)
                    make_pick(0)
                    make_bsel(0)
                    take_gather(r * E)
                    run_experts(dve, expert_dve, r)
                dve.wait_ge(combined, 4 * ROUNDS * E)
            def final_var(t):
                dve.wait_ge(sumsq_ready, 2 * T + 2 * t + 2)
                nc.vector.tensor_scalar(stat[:, 2 + t:3 + t], stat[:, 32 + 2 * t:33 + 2 * t], RMS_EPS,
                                        stat[:, 33 + 2 * t:34 + 2 * t], ALU.add, ALU.add).then_inc(var_ready, 1)

            def final_reciprocal(t):
                dve.wait_ge(std_ready, 4 + t)
                link(nc.vector.reciprocal(stat[:, 6 + t:7 + t], stat[:, 4 + t:5 + t]))

            def final_norm(t, half):
                cols = half_cols(half)
                nc.vector.scalar_tensor_tensor(resid[:, t, cols], resid[:, t, cols], stat[:, 6 + t:7 + t],
                                               fnw[:, cols], ALU.mult, ALU.mult).then_inc(out_ready, 1)

            dve.wait_ge(pick_ready, E)
            for k in range(2 * T):
                t, half = k // 2, k % 2
                dve.wait_ge(combined, 4 * E - 3 + k)
                nc.vector.tensor_tensor(resid[:, t, half_cols(half)], resid[:, t, half_cols(half)],
                                        bank(2 + 4 * t + half), ALU.add).then_inc(final_ready, 1)
                if k == 2:
                    final_var(0)
            final_reciprocal(0)
            dve.wait_ge(fnw_in, 16)
            final_norm(0, 0)
            final_var(1)
            final_norm(0, 1)
            final_reciprocal(1)
            final_norm(1, 0)
            final_norm(1, 1)

        @block.tensor
        def _(pe):
            mm = nc.tensor.matmul

            def keep_warm(times):
                for _ in range(times):
                    mm(bank(5)[:, 0:2 * P], warm_w[:, 0:P], warm_w[:, :], start=True, stop=True)

            pe.wait_ge(warm_w_ready, 1)
            keep_warm(WARM_X)
            pe.wait_ge(ident_in, 16)
            for b in range(4):
                t, c0 = b // 2, 4 * (b % 2)
                pe.wait_ge(x_in[t], 16)
                for c in range(4):
                    last = nc.tensor.transpose(bank(b)[:, c * P:(c + 1) * P],
                                               resid[:, t, (c0 + c) * P:(c0 + c + 1) * P], ident)
                last.then_inc(xT_done, 1)
            keep_warm(WARM_WIN)

            def project(j):
                pe.wait_ge(slot_full[j], 16)
                if j >= 2:
                    pe.wait_ge(nat_ready, j - 1)
                w = ring[:, j, :].rearrange("p (c n) -> p c n", c=C)
                for t in range(T):
                    if j == 0:
                        pe.wait_ge(hT_ready, 2 * t + 2)
                    for c in range(C):
                        last = mm(bank(4 + j % 2)[:, t * WIN_COLS:(t + 1) * WIN_COLS], hT[:, t, c, :], w[:, c, :],
                                  start=(c == 0), stop=(c == C - 1))
                last.then_inc(chunk_used, 1)

            def transpose_qk(i, j, nr):
                pe.wait_ge(roped, nr)
                if i:
                    pe.wait_ge(qkT_ready, i)
                for a in range(2):
                    for t in range(T):
                        last = nc.tensor.transpose(bank(6)[:, a * SEQ + t * P:a * SEQ + (t + 1) * P],
                                                   nat[:, t, CHUNK_COL[j] + a * P:CHUNK_COL[j] + (a + 1) * P], ident)
                last.then_inc(qkT_done, 1)

            def scores(g):
                pair = (2 * g, 2 * g + 1)
                rows = [slice(0, 64), slice(64, 128)]
                if g:
                    pe.wait_ge(masked, 2 * g)
                for h in pair:
                    q, k = qkT[rows[h % 2], 4 + h // 2, :], qkT[rows[h % 2], 8 + h // 2, :]
                    mm(bank(h % 2)[:, 0:P], q[:, 0:P], k[:, 0:P], start=True, stop=True)
                for h in pair:
                    q, k = qkT[rows[h % 2], 4 + h // 2, :], qkT[rows[h % 2], 8 + h // 2, :]
                    mm(bank(h % 2)[:, P:3 * P], q[:, P:SEQ], k, start=True, stop=True).then_inc(score_done, 1)

            def transpose_prob(g):
                for h in (2 * g, 2 * g + 1):
                    pe.wait_ge(prob_ready, h + 1)
                    for b in range(3):
                        last = nc.tensor.transpose(bank(2 if h % 2 == 0 else 7)[:, b * P:(b + 1) * P],
                                                   prob[:, h % 2, b * P:(b + 1) * P], ident)
                    last.then_inc(probT_done, 1)

            def prob_v(g):
                pe.wait_ge(nat_ready, 6)
                if g:
                    pe.wait_ge(pv_taken, g)
                pe.wait_ge(probT_ready, 2 * g + 2)
                for a, b, key, block, first, end in ((0, P, 0, 0, True, True), (P, SEQ, 0, 1, True, False),
                                                     (P, SEQ, 1, 2, False, True)):
                    for h in (2 * g, 2 * g + 1):
                        v = nat[:, key, MV + h * MOBA_DH:MV + (h + 1) * MOBA_DH]
                        last = mm(bank(3)[64 * (h % 2):64 * (h % 2) + 64, a:b], v,
                                  probT[:, h % 2, block * P:(block + 1) * P], start=first, stop=end)
                last.then_inc(pv_done, 1)

            def ret_scores(g):
                if g:
                    pe.wait_ge(decayed_ready, 2 * g)
                for h in (2 * g, 2 * g + 1):
                    r = slice(64 * (h % 2), 64 * (h % 2) + 64)
                    mm(bank(6 + h % 2)[:, 0:SEQ], qkT[r, 2 + h // 2, 0:P], qkT[r, h // 2, :], start=True, stop=True)
                for h in (2 * g, 2 * g + 1):
                    r = slice(64 * (h % 2), 64 * (h % 2) + 64)
                    mm(bank(6 + h % 2)[:, SEQ:SEQ + P], qkT[r, 2 + h // 2, P:SEQ], qkT[r, h // 2, P:SEQ],
                       start=True, stop=True).then_inc(rscore_done, 1)

            def ret_v(h):
                pe.wait_ge(decayed_ready, h + 1)
                cols = slice(h * RET_DV, (h + 1) * RET_DV)
                v = nat[:, :, RV + h * RET_DV:RV + (h + 1) * RET_DV]
                mm(bank(0)[:, cols], decayed[:, h % 2, 0:P], v[:, 0, :], start=True, stop=True)
                mm(bank(1)[:, cols], decayed[:, h % 2, P:2 * P], v[:, 0, :], start=True, stop=False)
                mm(bank(1)[:, cols], decayed[:, h % 2, 2 * P:3 * P], v[:, 1, :], start=False,
                   stop=True).then_inc(ret_done, 1)

            project(0)
            project(1)
            transpose_qk(0, 0, 1)
            project(2)
            transpose_qk(1, 1, 2)
            project(3)
            transpose_qk(2, 2, 3)
            project(4)
            transpose_qk(3, 3, 4)
            project(5)
            pe.wait_ge(qkT_ready, 4)
            scores(0)
            project(6)
            transpose_prob(0)
            scores(1)
            project(7)
            transpose_qk(4, 6, 5)
            prob_v(0)
            transpose_prob(1)
            scores(2)
            project(8)
            transpose_qk(5, 7, 6)
            prob_v(1)
            transpose_prob(2)
            scores(3)
            project(9)
            prob_v(2)
            transpose_prob(3)
            project(10)
            prob_v(3)
            pe.wait_ge(qkT_ready, 6)
            pe.wait_ge(probT_ready, MOBA_HEADS)
            ret_scores(0)
            project(11)
            pe.wait_ge(masked, MOBA_HEADS)
            ret_v(0)
            ret_v(1)
            ret_scores(1)

            def wout(s, c, t):
                w = ring[:, WIN_CHUNKS + s, :].rearrange("p (c n) -> p c n", c=2)
                for j in range(2):
                    last = mm(bank(2 + 4 * t + j), mixT[:, c, t * P:(t + 1) * P], w[:, c % 2, j * BANK:(j + 1) * BANK],
                              start=(c == 4), stop=(c == 3))
                return last

            def transpose_ret():
                pe.wait_ge(nat_ready, WIN_CHUNKS)
                pe.wait_ge(ret_ready, T)
                for i in range(2):
                    for a in range(2):
                        for t in range(T):
                            cols = (2 * i + a) * P
                            last = nc.tensor.transpose(bank(4 + i)[:, a * SEQ + t * P:a * SEQ + (t + 1) * P],
                                                       ret[:, t, cols:cols + P], ident)
                    last.then_inc(retT_done, 1)

            pe.wait_ge(pv_taken, 4)
            for s, pair in enumerate(WOUT_ORDER[0:2]):
                pe.wait_ge(slot_full[WIN_CHUNKS + s], 16)
                for c in (2 * pair, 2 * pair + 1):
                    for t in range(T):
                        if s == 1 and c % 2 == 1 and t == 1:
                            transpose_ret()
                        last = wout(s, c, t)
                        if s == 0 and c % 2 == 0 and t == 0:
                            ret_v(2)
                            ret_v(3)
                last.then_inc(chunk_used, 1)
            pe.wait_ge(retT_ready, 2)
            for s in (2, 3):
                pe.wait_ge(slot_full[WIN_CHUNKS + s], 16)
            for t in range(T):
                for s in (2, 3):
                    for c in (2 * WOUT_ORDER[s], 2 * WOUT_ORDER[s] + 1):
                        last = wout(s, c, t)
                    if t == T - 1:
                        last.then_inc(chunk_used, 1)
                if t == 0:
                    last.then_inc(wout_done, 1)

            before_w, ones_w = count_w[:, 0:P], count_w[:, P:2 * P]

            for t in range(T):
                pe.wait_ge(x2_ready, t + 1)
                for b in range(2):
                    for c in range(4):
                        last = nc.tensor.transpose(bank(6 * t + b)[:, c * P:(c + 1) * P],
                                                   resid[:, t, (4 * b + c) * P:(4 * b + c + 1) * P], ident)
                    last.then_inc(h2T_done, 1)
            pe.wait_ge(wr_ready, 1)
            for t in range(T):
                pe.wait_ge((h2T0_ready, h2T1_ready)[t], 2)
                for c in range(C):
                    g = c % 4
                    last = mm(bank(LT_BANK[t])[g * E:(g + 1) * E, 0:P], wr[:, c, :], h2T[:, t, c, :],
                              start=(c < 4), stop=(c >= 4))
                last.then_inc(lT_done, 1)
                keep_warm(3)
            for t in range(T):
                pe.wait_ge(lT_ready, t + 1)
                mm(bank(LOGIT_BANK[t])[:, 0:E], lT[:, t, :], row_id, start=True, stop=True).then_inc(logits_done, 1)
            keep_warm(WARM_TOPK)
            pe.wait_ge(member_ready, 1)
            mm(bank(2)[:, 0:E], before_w, member[:, 0, :], start=True, stop=True)
            mm(bank(2)[:, E:2 * E], ones_w, member[:, 0, :], start=True, stop=False)
            mm(bank(2)[:, E:2 * E], before_w, member[:, 1, :], start=False, stop=True)
            mm(bank(2)[:, 2 * E:3 * E], ones_w, member[:, 0, :], start=True, stop=False)
            mm(bank(2)[:, 2 * E:3 * E], ones_w, member[:, 1, :], start=False, stop=True).then_inc(prefix_done, 1)
            keep_warm(WARM_PLACE)

            def put_transposes(n):
                pe.wait_ge(pickg_ready, n)
                for t in range(T):
                    last = nc.tensor.transpose(bank(4)[:, t * P:(t + 1) * P], pickg[:, t, :], ident)
                last.then_inc(put_done, 1)

            def gather_tile(out, c):
                for t in range(T):
                    last = mm(out, resid[:, t, c * P:(c + 1) * P], pick[:, t, :], start=(t == 0), stop=(t == T - 1))
                return last

            def gather(n):
                pe.wait_ge(pick_ready, n + 1)
                for c in range(C):
                    last = gather_tile(bank(4)[:, c * SLOTS:(c + 1) * SLOTS], c)
                last.then_inc(gather_done, 1)

            def combine(n):
                pe.wait_ge(y_ready, n)
                for t in range(T):
                    for half in range(2):
                        rows = slice(64 * half, 64 * half + 64)
                        last = mm(bank(2 + 4 * t + half), putb[rows, t * P:(t + 1) * P], y_sb[rows, :],
                                  start=False, stop=False, skip_group_check=True)
                        last.then_inc(combined, 1)

            def expert_pe(r, i, j):
                n = r * E + local_expert(i, j)
                first = isinstance(r, int) and j == 0
                if first:
                    pe.wait_ge(gh0_ready, 1)
                else:
                    pe.wait_ge(gh_ready, n + 1)
                if j > 0:
                    put_transposes(n)
                for v in range(2):
                    for half in range(2):
                        mm(bank(v)[64 * half:64 * half + 64, :], bsel[v * E:(v + 1) * E, :],
                           b1_sb[v * E:(v + 1) * E, half * BANK:(half + 1) * BANK], start=True, stop=False)
                for k in range(W1_CHUNKS):
                    s = slot_of(j, k)
                    pe.wait_ge(slot_full[s], slot_count(r, i, j, k))
                    if first and k == C // 2:
                        pe.wait_ge(gh_ready, 1)
                        transpose_gates()
                    for v in range(2):
                        for half in range(2):
                            last = mm(bank(v)[64 * half:64 * half + 64, :], gh[:, k, :],
                                      ring[:, s, v * F + half * BANK:v * F + (half + 1) * BANK],
                                      start=False, stop=(k == W1_CHUNKS - 1))
                    last.then_inc(chunk_used, 1)
                if j > 0:
                    pe.wait_ge(put_ready, n)
                if j < LAST:
                    gather(n + 1)
                if j > 0:
                    combine(n)
                if first:
                    start_accumulators()
                if j == LAST:
                    put_transposes(n + 1)
                pe.wait_ge(act_ready, n + 1)
                for c in range(4):
                    last = nc.tensor.transpose(bank(5)[:, c * P:(c + 1) * P], a_sb[:, c * P:(c + 1) * P], ident)
                last.then_inc(actT_done, 1)
                pe.wait_ge(actT_ready, n + 1)
                for k in range(W2_CHUNKS):
                    s = slot_of(j, W1_CHUNKS + k)
                    pe.wait_ge(slot_full[s], slot_count(r, i, j, W1_CHUNKS + k))
                    for c in (2 * k, 2 * k + 1):
                        for half in range(2):
                            last = mm(bank(5)[64 * half:64 * half + 64, :],
                                      aT[:, c % 4, 64 * (c // 4):64 * (c // 4) + 64],
                                      ring[:, s, (c % 2) * D + half * BANK:(c % 2) * D + (half + 1) * BANK],
                                      start=(c == 0), stop=(c == C - 1))
                    last.then_inc(chunk_used, 1)
                if j == LAST:
                    pe.wait_ge(put_ready, n + 1)
                    combine(n + 1)

            def transpose_gates():
                pe.wait_ge(most_ready, 1)
                for t in range(T):
                    last = nc.tensor.transpose(bank(7)[0:E, t * P:(t + 1) * P], gates[:, t, 0:E], ident)
                last.then_inc(gatesT_done, 1)

            def start_accumulators():
                pe.wait_ge(gatesT_ready, 1)
                for t in range(T):
                    for half in range(2):
                        mm(bank(2 + 4 * t + half), gatesT[:, t * P:(t + 1) * P], b2_sb[:, half * BANK:(half + 1) * BANK],
                           start=True, stop=False, skip_group_check=True)

            pe.wait_ge(pick_ready, 1)
            for half in range(2):
                for c in range(4):
                    last = gather_tile(bank(4 + half)[:, c * SLOTS:(c + 1) * SLOTS], 4 * half + c)
                last.then_inc(gather0_done, 1)
            pe.wait_ge(late_in, 48)
            run_experts(pe, expert_pe, 0)
            most_v = pe.value_load(most_i[0:1, 0:1], min_val=0, max_val=SEQ)
            with pe.If(most_v > SLOTS):
                with pe.Fori(1, ROUNDS) as r:
                    gather(r * E)
                    run_experts(pe, expert_pe, r)


def constants():
    import numpy as np
    f = np.float32
    p = np.arange(P)
    part = {}
    part["ident"] = np.eye(P)
    part["before"] = p[:, None] < p[None, :]
    part["ones"] = np.ones((P, P))
    part["causal"] = np.where(p[None, :] <= p[:, None], 0.0, -1e30)
    log_g = np.log1p(-np.exp2(f(-5.0) - np.arange(RET_HEADS, dtype=f)))
    rel = (np.arange(SEQ)[None, :] - p[:, None]).astype(f)
    dec = np.where(rel >= 0, np.exp(log_g[:, None, None] * np.maximum(rel, 0)), 0) * f(RET_DK ** -0.5)
    part["decay"] = dec.transpose(1, 0, 2).reshape(P, -1)
    part["slot"] = np.tile(np.arange(SLOTS), (P, 2))
    part["row"] = p[:, None] % E == np.arange(E)[None, :]
    for name, dim, theta in (("ret", RET_DK, 10000.0), ("moba", MOBA_ROPE, 500000.0)):
        half = dim // 2
        inv = f(theta) ** (f(-2.0) * np.arange(half, dtype=f) / f(dim))
        ang = np.arange(SEQ, dtype=f)[:, None] * inv[None, :].astype(f)
        cos, sin = np.cos(ang), np.sin(ang)
        for which, tab in (("cos", np.concatenate([cos, cos], 1)), ("sin", np.concatenate([-sin, sin], 1))):
            part[f"{name}_{which}"] = tab.reshape(T, P, dim).transpose(1, 0, 2).reshape(P, -1)
    return np.concatenate([part[n].astype(f) for n, _ in CONST_PARTS], axis=1)


_INS = ["x", "norm1_w", "w_in", "ret_norm_w", "w_out", "norm2_w", "w_router", "b_router",
        "w1", "b1", "w2", "b2", "final_norm_w"]


def kernel(**inputs):
    import numpy as np
    import concourse.bacc as bacc
    from concourse.bass_utils import run_bass_kernel_spmd

    nc = bacc.Bacc("TRN2", target_bir_lowering=False, num_devices=1)
    arrays, args = {}, []
    for name, a in [(n, inputs[n]) for n in _INS] + [("consts", constants())]:
        a = np.ascontiguousarray(a)
        arrays[f"in_{name}"] = a
        args.append(nc.dram_tensor(f"in_{name}", a.shape, mybir.dt.from_np(a.dtype), kind="ExternalInput").ap())
    args.append(nc.dram_tensor("out_0", (1, SEQ, D), F32, kind="ExternalOutput").ap())
    layer_kernel(nc, *args)
    r = run_bass_kernel_spmd(nc, [arrays], core_ids=[0])
    return r.results[0]["out_0"]
```
